# Optimizing a Trainium2 kernel written in Bass

```python
import jax
import jax.numpy as jnp
from jax import lax
import numpy as np

D_MODEL = 1024
BATCH = 1
SEQ = 256
DEPTH = 2

N_BRANCH = 4
ROPE_THETA = 500000.0
NORM_EPS = 1e-6
NEG_INF = -1e30
QBLOCK = 128
MAX_POS_OFFSET = 1024

A_GROUPS = 4
A_GROUP_DIM = 64
A_WIDTH = A_GROUPS * A_GROUP_DIM
A_CHUNK = 128
B_HEADS = 4
B_HEAD_DIM = 64
B_WIDTH = B_HEADS * B_HEAD_DIM
B_ROT_DIM = B_HEAD_DIM // 4
MOBA_BLOCK = 256
MOBA_TOPK = 3
MOBA_QCHUNK = 64
C_HEADS = 4
C_Q_RANK = 192
C_KV_RANK = 128
C_NOPE_DIM = 64
C_ROPE_DIM = 32
C_V_DIM = 64
C_QK_DIM = C_NOPE_DIM + C_ROPE_DIM
C_WIDTH = C_HEADS * C_V_DIM
D_WIDTH = 256
D_CONV = 31
FFN_DIM = 2816
N_EXPERTS = 8
TOP_K = 2
EXPERT_DIM = 1408
EXPERT_ROWS = 512
N_DENSE = (DEPTH + 1) // 2
N_MOE = DEPTH // 2

GATE_COLS = N_BRANCH * D_MODEL
A_COLS = 2 * A_WIDTH
B_COLS = 3 * B_WIDTH
C_COLS = C_Q_RANK + C_KV_RANK + C_ROPE_DIM
D_COLS = 2 * D_WIDTH
IN_COLS = GATE_COLS + A_COLS + B_COLS + C_COLS + D_COLS
IN_SPLITS = [GATE_COLS, GATE_COLS + A_COLS, GATE_COLS + A_COLS + B_COLS, GATE_COLS + A_COLS + B_COLS + C_COLS]

kernel_name = 'hybrid_gated_gmlp_moba_mla_conv_moe_trunk'

def rmsnorm(x, g):
    xf = x.astype(jnp.float32)
    y = xf * lax.rsqrt(jnp.mean(xf * xf, axis=-1, keepdims=True) + NORM_EPS)
    return (y * g.astype(jnp.float32)).astype(x.dtype)

def layernorm(x, g, b):
    xf = x.astype(jnp.float32)
    mu = jnp.mean(xf, axis=-1, keepdims=True)
    xc = xf - mu
    y = xc * lax.rsqrt(jnp.mean(xc * xc, axis=-1, keepdims=True) + NORM_EPS)
    return (y * g.astype(jnp.float32) + b.astype(jnp.float32)).astype(x.dtype)

def rope(x, pos):
    r = x.shape[-1]
    inv = jnp.float32(ROPE_THETA) ** (-jnp.arange(0, r, 2, dtype=jnp.float32) / r)
    ang = pos.astype(jnp.float32)[:, :, None, None] * inv
    cos, sin = jnp.cos(ang), jnp.sin(ang)
    xf = x.astype(jnp.float32)
    x1, x2 = xf[..., : r // 2], xf[..., r // 2:]
    return jnp.concatenate([x1 * cos - x2 * sin, x2 * cos + x1 * sin], axis=-1).astype(x.dtype)

def dense_causal_attention(q, k, v):
    _, S, _, dk = q.shape
    scale = dk ** -0.5
    outs = []
    for i in range(S // QBLOCK):
        lo, hi = i * QBLOCK, (i + 1) * QBLOCK
        s = jnp.einsum('bqhd,bkhd->bhqk', q[:, lo:hi], k[:, :hi]).astype(jnp.float32) * scale
        causal = jnp.arange(hi)[None, :] <= jnp.arange(lo, hi)[:, None]
        p = jax.nn.softmax(jnp.where(causal, s, NEG_INF), axis=-1).astype(v.dtype)
        outs.append(jnp.einsum('bhqk,bkhd->bqhd', p, v[:, :hi]))
    return jnp.concatenate(outs, axis=1)

def moba_attention(q, k, v):
    B, S, H, D = q.shape
    nb = -(-S // MOBA_BLOCK)
    sp = nb * MOBA_BLOCK
    pad = [(0, 0), (0, sp - S), (0, 0), (0, 0)]
    q = jnp.pad(q, pad).transpose(0, 2, 1, 3)
    k = jnp.pad(k, pad).transpose(0, 2, 1, 3)
    v = jnp.pad(v, pad).transpose(0, 2, 1, 3)
    kb = k.reshape(B, H, nb, MOBA_BLOCK, D)
    vb = v.reshape(B, H, nb, MOBA_BLOCK, D)
    k_mean = jnp.mean(kb.astype(jnp.float32), axis=3)
    q_block = jnp.arange(sp) // MOBA_BLOCK
    score = jnp.einsum('bhsd,bhnd->bhsn', q.astype(jnp.float32), k_mean)
    past = jnp.arange(nb)[None, :] < q_block[:, None]
    score = jnp.where(past, score, NEG_INF)
    n_sel = min(MOBA_TOPK, nb)
    _, sel = lax.top_k(score, n_sel)
    sel_ok = sel < q_block[None, None, :, None]
    bi = jnp.arange(B)[:, None, None, None]
    hi = jnp.arange(H)[None, :, None, None]
    scale = D ** -0.5

    def chunk(c):
        start = c * MOBA_QCHUNK
        qc = lax.dynamic_slice_in_dim(q, start, MOBA_QCHUNK, axis=2)
        idx = lax.dynamic_slice_in_dim(sel, start, MOBA_QCHUNK, axis=2)
        ok = lax.dynamic_slice_in_dim(sel_ok, start, MOBA_QCHUNK, axis=2)
        kg = kb[bi, hi, idx]
        vg = vb[bi, hi, idx]
        own = start // MOBA_BLOCK
        ko = lax.dynamic_index_in_dim(kb, own, axis=2, keepdims=False)
        vo = lax.dynamic_index_in_dim(vb, own, axis=2, keepdims=False)
        s_sel = jnp.einsum('bhqd,bhqnkd->bhqnk', qc, kg).astype(jnp.float32) * scale
        s_sel = jnp.where(ok[..., None], s_sel, NEG_INF).reshape(B, H, MOBA_QCHUNK, n_sel * MOBA_BLOCK)
        s_own = jnp.einsum('bhqd,bhkd->bhqk', qc, ko).astype(jnp.float32) * scale
        qpos = start + jnp.arange(MOBA_QCHUNK)[:, None]
        kpos = own * MOBA_BLOCK + jnp.arange(MOBA_BLOCK)[None, :]
        s_own = jnp.where(kpos <= qpos, s_own, NEG_INF)
        p = jax.nn.softmax(jnp.concatenate([s_sel, s_own], axis=-1), axis=-1).astype(v.dtype)
        p_sel = p[..., : n_sel * MOBA_BLOCK].reshape(B, H, MOBA_QCHUNK, n_sel, MOBA_BLOCK)
        p_own = p[..., n_sel * MOBA_BLOCK:]
        return (jnp.einsum('bhqnk,bhqnkd->bhqd', p_sel, vg)
                + jnp.einsum('bhqk,bhkd->bhqd', p_own, vo))

    out = lax.map(chunk, jnp.arange(sp // MOBA_QCHUNK))
    out = out.transpose(1, 0, 3, 2, 4).reshape(B, sp, H, D)
    return out[:, :S]

def chunked_sgu(u, v, ln_g, ln_b, w_s, b_s):
    B, S, _ = v.shape
    v = layernorm(v, ln_g, ln_b).reshape(B, S // A_CHUNK, A_CHUNK, A_GROUPS, A_GROUP_DIM)
    causal = jnp.tril(jnp.ones((A_CHUNK, A_CHUNK), w_s.dtype))
    z = jnp.einsum('gts,bcsgd->bctgd', w_s * causal, v) + b_s.T[None, None, :, :, None]
    return u * z.reshape(B, S, A_WIDTH)

def mla_attention(cq, ckv, kr, pos, cq_g, ckv_g, w_uq, w_ukv, qn_g, kn_g):
    B, S, _ = cq.shape
    q = (rmsnorm(cq, cq_g) @ w_uq).reshape(B, S, C_HEADS, C_QK_DIM)
    kv = (rmsnorm(ckv, ckv_g) @ w_ukv).reshape(B, S, C_HEADS, C_NOPE_DIM + C_V_DIM)
    k_nope, v = kv[..., :C_NOPE_DIM], kv[..., C_NOPE_DIM:]
    k_rope = jnp.broadcast_to(kr[:, :, None, :], (B, S, C_HEADS, C_ROPE_DIM))
    k = jnp.concatenate([k_nope, k_rope], axis=-1)
    q = rmsnorm(q, qn_g)
    k = rmsnorm(k, kn_g)
    q = jnp.concatenate([q[..., :C_NOPE_DIM], rope(q[..., C_NOPE_DIM:], pos)], axis=-1)
    k = jnp.concatenate([k[..., :C_NOPE_DIM], rope(k[..., C_NOPE_DIM:], pos)], axis=-1)
    return dense_causal_attention(q, k, v).reshape(B, S, C_WIDTH)

def conformer_conv(a, g, conv_w, conv_b, ln_g, ln_b):
    z = a * jax.nn.sigmoid(g)
    z = lax.conv_general_dilated(z, conv_w[:, None, :], window_strides=(1,),
                                 padding=[(D_CONV - 1, 0)],
                                 dimension_numbers=('NWC', 'WIO', 'NWC'),
                                 feature_group_count=D_WIDTH) + conv_b
    return jax.nn.silu(layernorm(z, ln_g, ln_b))

def hybrid_mixer(h, pos, w_in, a_ln_g, a_ln_b, a_ws, a_bs, b_qn, b_kn, c_cq_norm, c_ckv_norm,
                 c_w_uq, c_w_ukv, c_qn, c_kn, d_conv_w, d_conv_b, d_ln_g, d_ln_b, w_branch, w_out):
    B, S, _ = h.shape
    proj = h @ w_in
    gates, pa, pb, pc, pd = jnp.split(proj, IN_SPLITS, axis=-1)
    u, v = jnp.split(pa, 2, axis=-1)
    o_a = chunked_sgu(u, v, a_ln_g, a_ln_b, a_ws, a_bs)
    qkv = pb.reshape(B, S, 3, B_HEADS, B_HEAD_DIM)
    qb = rmsnorm(qkv[:, :, 0], b_qn)
    kb = rmsnorm(qkv[:, :, 1], b_kn)
    qb = jnp.concatenate([rope(qb[..., :B_ROT_DIM], pos), qb[..., B_ROT_DIM:]], axis=-1)
    kb = jnp.concatenate([rope(kb[..., :B_ROT_DIM], pos), kb[..., B_ROT_DIM:]], axis=-1)
    o_b = moba_attention(qb, kb, qkv[:, :, 2]).reshape(B, S, B_WIDTH)
    cq, ckv, kr = jnp.split(pc, [C_Q_RANK, C_Q_RANK + C_KV_RANK], axis=-1)
    o_c = mla_attention(cq, ckv, kr, pos, c_cq_norm, c_ckv_norm, c_w_uq, c_w_ukv, c_qn, c_kn)
    da, dg = jnp.split(pd, 2, axis=-1)
    o_d = conformer_conv(da, dg, d_conv_w, d_conv_b, d_ln_g, d_ln_b)
    y = sum(jax.nn.sigmoid(gates[..., n * D_MODEL:(n + 1) * D_MODEL]) * (o @ w_branch[n])
            for n, o in enumerate((o_a, o_b, o_c, o_d)))
    return y @ w_out

def swiglu(h, w_gate, w_up, w_down):
    return (jax.nn.silu(h @ w_gate) * (h @ w_up)) @ w_down

def moe_swiglu(h, w_router, b_router, w_gate, w_up, w_down):
    B, S, D = h.shape
    T = B * S
    TK = T * TOP_K
    xt = h.reshape(T, D)
    logits = (xt @ w_router).astype(jnp.float32) + b_router.astype(jnp.float32)
    top_logit, top_e = lax.top_k(logits, TOP_K)
    top_w = jax.nn.softmax(top_logit, axis=-1)
    flat_e = top_e.reshape(TK)
    flat_tok = jnp.repeat(jnp.arange(T, dtype=jnp.int32), TOP_K)
    flat_w = top_w.reshape(TK)
    order = jnp.argsort(flat_e)
    sorted_e = flat_e[order]
    counts = jnp.bincount(flat_e, length=N_EXPERTS)
    starts = jnp.cumsum(counts) - counts
    padded = (counts + EXPERT_ROWS - 1) // EXPERT_ROWS * EXPERT_ROWS
    pends = jnp.cumsum(padded)
    pstarts = pends - padded
    dest = pstarts[sorted_e] + jnp.arange(TK) - starts[sorted_e]
    n_blocks = -(-TK // EXPERT_ROWS) + N_EXPERTS
    rows = n_blocks * EXPERT_ROWS
    row_tok = jnp.zeros((rows,), jnp.int32).at[dest].set(flat_tok[order])
    row_w = jnp.zeros((rows,), jnp.float32).at[dest].set(flat_w[order])
    block_e = jnp.minimum(jnp.searchsorted(pends, jnp.arange(n_blocks) * EXPERT_ROWS, side='right'),
                          N_EXPERTS - 1)
    xs = xt[row_tok].reshape(n_blocks, EXPERT_ROWS, D)

    def expert_block(args):
        xb, e = args
        return (jax.nn.silu(xb @ w_gate[e]) * (xb @ w_up[e])) @ w_down[e]

    ys = lax.map(expert_block, (xs, block_e)).reshape(rows, D)
    out = jnp.zeros((T, D), h.dtype).at[row_tok].add(ys * row_w[:, None].astype(ys.dtype))
    return out.reshape(B, S, D)

def setup_inputs(seed: int = 0) -> dict:
    key = jax.random.key(seed)
    ks = jax.random.split(key, 32)
    f32 = jnp.float32

    def nrm(k, shape, fan_in):
        return jax.random.normal(k, shape, f32) * (fan_in ** -0.5)

    def gain(k, shape):
        return 1.0 + 0.02 * jax.random.normal(k, shape, f32)

    def small(k, shape, s=0.02):
        return s * jax.random.normal(k, shape, f32)

    x = jax.random.normal(ks[0], (BATCH, SEQ, D_MODEL), f32)
    offset = jax.random.randint(ks[1], (BATCH, 1), 0, MAX_POS_OFFSET, dtype=jnp.int32)
    positions = offset + jnp.arange(SEQ, dtype=jnp.int32)[None, :]
    return {
        'x': x,
        'positions': positions,
        'attn_norm': gain(ks[2], (DEPTH, D_MODEL)),
        'ffn_norm': gain(ks[3], (DEPTH, D_MODEL)),
        'w_in': nrm(ks[4], (DEPTH, D_MODEL, IN_COLS), D_MODEL),
        'a_ln_g': gain(ks[5], (DEPTH, A_WIDTH)),
        'a_ln_b': small(ks[6], (DEPTH, A_WIDTH)),
        'a_ws': nrm(ks[7], (DEPTH, A_GROUPS, A_CHUNK, A_CHUNK), A_CHUNK),
        'a_bs': gain(ks[8], (DEPTH, A_GROUPS, A_CHUNK)),
        'b_qn': gain(ks[9], (DEPTH, B_HEAD_DIM)),
        'b_kn': gain(ks[10], (DEPTH, B_HEAD_DIM)),
        'c_cq_norm': gain(ks[11], (DEPTH, C_Q_RANK)),
        'c_ckv_norm': gain(ks[12], (DEPTH, C_KV_RANK)),
        'c_w_uq': nrm(ks[13], (DEPTH, C_Q_RANK, C_HEADS * C_QK_DIM), C_Q_RANK),
        'c_w_ukv': nrm(ks[14], (DEPTH, C_KV_RANK, C_HEADS * (C_NOPE_DIM + C_V_DIM)), C_KV_RANK),
        'c_qn': gain(ks[15], (DEPTH, C_QK_DIM)),
        'c_kn': gain(ks[16], (DEPTH, C_QK_DIM)),
        'd_conv_w': nrm(ks[17], (DEPTH, D_CONV, D_WIDTH), D_CONV),
        'd_conv_b': small(ks[18], (DEPTH, D_WIDTH)),
        'd_ln_g': gain(ks[19], (DEPTH, D_WIDTH)),
        'd_ln_b': small(ks[20], (DEPTH, D_WIDTH)),
        'w_branch': nrm(ks[21], (DEPTH, N_BRANCH, A_WIDTH, D_MODEL), A_WIDTH),
        'w_out': nrm(ks[22], (DEPTH, D_MODEL, D_MODEL), D_MODEL),
        'ffn_w_gate': nrm(ks[23], (N_DENSE, D_MODEL, FFN_DIM), D_MODEL),
        'ffn_w_up': nrm(ks[24], (N_DENSE, D_MODEL, FFN_DIM), D_MODEL),
        'ffn_w_down': nrm(ks[25], (N_DENSE, FFN_DIM, D_MODEL), FFN_DIM),
        'moe_router': nrm(ks[26], (N_MOE, D_MODEL, N_EXPERTS), D_MODEL),
        'moe_router_b': small(ks[27], (N_MOE, N_EXPERTS), 0.01),
        'moe_w_gate': nrm(ks[28], (N_MOE, N_EXPERTS, D_MODEL, EXPERT_DIM), D_MODEL),
        'moe_w_up': nrm(ks[29], (N_MOE, N_EXPERTS, D_MODEL, EXPERT_DIM), D_MODEL),
        'moe_w_down': nrm(ks[30], (N_MOE, N_EXPERTS, EXPERT_DIM, D_MODEL), EXPERT_DIM),
    }

def reference(x, positions, attn_norm, ffn_norm, w_in, a_ln_g, a_ln_b, a_ws, a_bs, b_qn, b_kn,
              c_cq_norm, c_ckv_norm, c_w_uq, c_w_ukv, c_qn, c_kn, d_conv_w, d_conv_b, d_ln_g, d_ln_b,
              w_branch, w_out, ffn_w_gate, ffn_w_up, ffn_w_down, moe_router, moe_router_b,
              moe_w_gate, moe_w_up, moe_w_down):
    for l in range(DEPTH):
        h = rmsnorm(x, attn_norm[l])
        x = x + hybrid_mixer(h, positions, w_in[l], a_ln_g[l], a_ln_b[l], a_ws[l], a_bs[l],
                             b_qn[l], b_kn[l], c_cq_norm[l], c_ckv_norm[l], c_w_uq[l], c_w_ukv[l],
                             c_qn[l], c_kn[l], d_conv_w[l], d_conv_b[l], d_ln_g[l], d_ln_b[l],
                             w_branch[l], w_out[l])
        h = rmsnorm(x, ffn_norm[l])
        i = l // 2
        if l % 2 == 0:
            x = x + swiglu(h, ffn_w_gate[i], ffn_w_up[i], ffn_w_down[i])
        else:
            x = x + moe_swiglu(h, moe_router[i], moe_router_b[i], moe_w_gate[i], moe_w_up[i],
                               moe_w_down[i])
    return x


_drawn_inputs = setup_inputs


def setup_inputs(seed=0):
    import zlib

    import numpy as np

    out = dict(_drawn_inputs(seed))
    spreads = {}
    factors = {'a_ln_g': 9.034,
     'a_ln_b': 9.214,
     'a_bs': 7.189,
     'b_qn': 5.128,
     'b_kn': 5.471,
     'c_cq_norm': 3.77,
     'c_ckv_norm': 7.962,
     'c_qn': 3.968,
     'c_kn': 5.464,
     'd_ln_g': 9.005,
     'd_ln_b': 10.974,
     'moe_router_b': 24.315,
     'ffn_norm': 3.992}
    for name, (base, spread) in spreads.items():
        noise = np.random.default_rng([zlib.crc32(name.encode()), seed]).standard_normal(out[name].shape)
        drawn = base * np.exp(spread * noise) if base else spread * noise
        out[name] = jnp.asarray(drawn.astype(out[name].dtype))
    for name, factor in factors.items():
        out[name] = (out[name] * factor).astype(out[name].dtype)
    return out
```

```python
from contextlib import ExitStack

import numpy as np
import concourse.bass as bass
from concourse import mybir

F32 = mybir.dt.float32
F32R = mybir.dt.float32r
I32 = mybir.dt.int32
U32 = mybir.dt.uint32
ALU = mybir.AluOpType
ACT = mybir.ActivationFunctionType
AX_X = mybir.AxisListType.X

P = 128
D = 1024
T = 256
MT = T // P
KD = D // P
DEPTH = 2
NB = 4
BW = 256
HEADS = 4
HD = 64
B_ROT = 16
CQ, CKV, CR = 192, 128, 32
C_QK = HD + CR
D_CONV = 31
FFN = 2816
NE = 8
EDIM = 1408
GATES = NB * D
REST = 2 * BW + 3 * BW + (CQ + CKV + CR) + 2 * BW
EPS = 1e-6
NEG = -1e30
THETA = 500000.0
A_U, A_V = 0, BW
B_Q, B_K, B_V = 2 * BW, 3 * BW, 4 * BW
C_Q = 5 * BW
C_R = C_Q + CQ + CKV
D_A = C_R + CR
D_G = D_A + BW

PIECE = 2048
HALF = PIECE // 2
RING = 3
ERING = 6
CHUNK_ORDER = [2, 3, 1, 4, 0]
WIDTHS = [min(512, REST - 512 * c) for c in range(5)]
MIX_PIECES = 33
FSTEP = 256
FSTEPS = FFN // FSTEP
FFN_BASE = MIX_PIECES
MOE_BASE = 2 * MIX_PIECES + 3 * FSTEPS
ESTEPS = [256] * 5 + [128]
PASS_PIECES = 18
SLOTS = 128
PASSES = 12

ORDER = [("g", 0), ("u", 0)]
for _s in range(1, 6):
    ORDER += [("g", _s), ("u", _s), ("d", _s - 1)]
ORDER += [("d", 5)]

INPUTS = ['x', 'positions', 'attn_norm', 'ffn_norm', 'w_in', 'a_ln_g', 'a_ln_b', 'a_ws', 'a_bs', 'b_qn', 'b_kn',
          'c_cq_norm', 'c_ckv_norm', 'c_w_uq', 'c_w_ukv', 'c_qn', 'c_kn', 'd_conv_w', 'd_conv_b', 'd_ln_g',
          'd_ln_b', 'w_branch', 'w_out', 'ffn_w_gate', 'ffn_w_up', 'ffn_w_down', 'moe_router', 'moe_router_b',
          'moe_w_gate', 'moe_w_up', 'moe_w_down']

N_PARAM = 17


def build_trunk(nc, a, out):
    with ExitStack() as ctx:
        base = (nc.sbuf_base + 63) // 64 * 64
        top = [base]

        def place(name, shape, dt=F32):
            n = 4 * int(np.prod(shape[1:]))
            t = nc.alloc_sbuf_tensor_at(name, shape, dt, offset=top[0])
            top[0] += (n + 31) // 32 * 32
            return t

        x = place("x", [P, MT, D])
        h = place("h", [P, MT * D])
        hTh = place("hTh", [P, KD, T], F32R)
        hTl = place("hTl", [P, KD, T], F32R)
        ring = [place(f"ring{i}", [P, PIECE]) for i in range(RING)]
        whi = [place(f"whi{i}", [P, HALF], F32R) for i in range(4)]
        wlo = [place(f"wlo{i}", [P, HALF], F32R) for i in range(4)]
        gain = place("gain", [P, D])
        ident = place("ident", [P, P])
        tri384 = place("tri384", [P, 384])
        upper = place("upper", [P, P])
        upstrict = place("upstrict", [P, P])
        ones = place("ones", [P, P])
        mean_w = place("mean_w", [P, P])
        eps = place("eps", [P, 1])
        wr = place("wr", [P, KD, NE])
        rbias = place("rbias", [P, NE])
        inv = place("inv", [P, 16])
        cosT = place("cosT", [P, MT, 16])
        sinT = place("sinT", [P, MT, 16])
        posi = place("posi", [P, MT], I32)
        posf = place("posf", [P, MT])
        ssum = place("ssum", [P, MT])
        rstd = place("rstd", [P, 2, MT])
        stat = place("stat", [P, 64])

        shared = top[0]
        gates = place("gates", [P, MT, GATES])
        prj = place("prj", [P, MT, REST])
        ctq = place("ctq", [P, MT, HEADS * C_QK])
        ckv = place("ckv", [P, MT, 512])
        qkT = place("qkT", [P, 2, HEADS, T])
        oTh = place("oTh", [P, NB, 2, T], F32R)
        oTl = place("oTl", [P, NB, 2, T], F32R)
        zpad = place("zpad", [P, 2, D_CONV - 1 + T])
        dacc = place("dacc", [P, 2, T])
        dxc = place("dxc", [P, 2, T])
        pT = place("pT", [P, HEADS, 384])
        wsT = place("wsT", [P, 4, P])
        cw = place("cw", [P, 2, D_CONV])
        uq = place("uq", [P, 2, HEADS * C_QK])
        ukv = place("ukv", [P, 512])
        wsr = place("wsr", [P, 4, P])
        cwr = place("cwr", [P, BW])
        bgain = place("bgain", [P, 2, HD])
        cqkgain = place("cqkgain", [P, 2, C_QK])
        cngain = place("cngain", [P, CQ + CKV])
        again = place("again", [P, 2, BW])
        dcol = place("dcol", [P, 3, 2])
        abs_ = place("abs_", [P, 4])
        end = top[0]

        top[0] = shared
        sig = place("sig", [P, MT, FSTEP])
        act = place("act", [P, MT, FSTEP])
        aTh = [place(f"aTh{i}", [P, 2, T], F32R) for i in range(2)]
        aTl = [place(f"aTl{i}", [P, 2, T], F32R) for i in range(2)]
        ering = ring + [place(f"ring{i}", [P, PIECE]) for i in range(RING, ERING)]
        htokh = place("htokh", [P, MT, D], F32R)
        htokl = place("htokl", [P, MT, D], F32R)
        xgh = place("xgh", [P, KD, P], F32R)
        xgl = place("xgl", [P, KD, P], F32R)
        yh = place("yh", [P, D], F32R)
        yl = place("yl", [P, D], F32R)
        pick = place("pick", [P, MT, P], F32R)
        pickf = place("pickf", [P, MT, P])
        pickT = place("pickT", [P, T], F32R)
        wcol = place("wcol", [P, MT])
        wslot = place("wslot", [P, 1])
        wrh = place("wrh", [P, KD, NE], F32R)
        wrl = place("wrl", [P, KD, NE], F32R)
        lg = place("lg", [P, MT, NE])
        top8 = place("top8", [P, MT, 8])
        idx8 = place("idx8", [P, MT, 8], U32)
        idxf = place("idxf", [P, MT, 2])
        wtop = place("wtop", [P, MT, 2])
        diff = place("diff", [P, MT, 2])
        hot = place("hot", [P, 2, MT, NE])
        tab = place("tab", [P, 6, PASSES])
        prod = place("prod", [P, 6, NE])
        cnt = place("cnt", [P, NE])
        over = place("over", [P, NE])
        oidx = place("oidx", [P, NE])
        sel = place("sel", [P, NE])
        iotai = place("iotai", [P, P], I32)
        iotaf = place("iotaf", [P, P])
        eidf = place("eidf", [P, PASSES])
        eidi = place("eidi", [P, PASSES], I32)
        lastf = place("lastf", [P, 1])
        lasti = place("lasti", [P, 1], I32)
        top[0] = max(end, top[0])
        assert top[0] <= nc.sbuf_usable_end, (top[0], nc.sbuf_usable_end)

        hm = h[:, :].rearrange("p (m d) -> p m d", m=MT)
        scr0, scr1 = h[:, 0:D], h[:, D:2 * D]
        probs = h[:, 0:HEADS * 384].rearrange("p (h k) -> p h k", h=HEADS)
        cT = pT[:, 0:2, :].rearrange("p h k -> p (h k)").rearrange("p (c t) -> p c t", t=T)
        dsd = pT[:, 3, 0:T]
        cn = scr1[:, 0:MT * 320].rearrange("p (m c) -> p m c", m=MT)
        kc = scr1[:, 0:MT * HEADS * C_QK].rearrange("p (m c) -> p m c", m=MT)

        bank = [ctx.enter_context(nc.psum_tensor(f"bank{i}", [P, 512], F32)) for i in range(8)]

        def sem(name):
            return ctx.enter_context(nc.semaphore(name))

        x_in = [sem(f"x_in{m}") for m in range(MT)]
        pos_in, iota_ready = sem("pos_in"), sem("iota_ready")
        out_done = sem("out_done")
        raw_in = [sem(f"raw_in{i}") for i in range(ERING)]
        hi_done, lo_done, w_used = sem("hi_done"), sem("lo_done"), sem("w_used")
        const_ready = sem("const_ready")
        pool_seq, dve_seq, act_seq = sem("pool_seq"), sem("dve_seq"), sem("act_seq")
        gain_in, gain_free = sem("gain_in"), sem("gain_free")
        param_in = sem("param_in")
        layer_done = sem("layer_done")
        x_new = sem("x_new")
        rms_sum, rms_root, h_ready = sem("rms_sum"), sem("rms_root"), sem("h_ready")
        hT_mm, hT_hi, hT_lo = sem("hT_mm"), sem("hT_hi"), sem("hT_lo")
        prj_ev = sem("prj_ev")
        wprep_mm, wprep_ev = sem("wprep_mm"), sem("wprep_ev")
        ang_ready, trig_ready = sem("ang_ready"), sem("trig_ready")
        cms, cms_root, cn_ready = sem("cms"), sem("cms_root"), sem("cn_ready")
        cnT_mm, cnT_ev = sem("cnT_mm"), sem("cnT_ev")
        up_mm, up_ev = sem("up_mm"), sem("up_ev")
        qms, qms_root, cqk_ready = sem("qms"), sem("qms_root"), sem("cqk_ready")
        bms, bms_root, bqk_ready = sem("bms"), sem("bms_root"), sem("bqk_ready")
        qT_mm, qT_evA, qT_evV = sem("qT_mm"), sem("qT_evA"), sem("qT_evV")
        sc_mm, sc_ev, mx_ready, ex_done, pn_ready = (sem("sc_mm"), sem("sc_ev"), sem("mx_ready"), sem("ex_done"),
                                                     sem("pn_ready"))
        pT_mm, pT_evA, pT_evV = sem("pT_mm"), sem("pT_evA"), sem("pT_evV")
        o_mm = [sem(f"o_mm{n}") for n in range(NB)]
        o_hi = [sem(f"o_hi{n}") for n in range(NB)]
        o_lo = [sem(f"o_lo{n}") for n in range(NB)]
        glu_sig, glu_ready, zT_mm = sem("glu_sig"), sem("glu_ready"), sem("zT_mm")
        ams, ams_root, vln_ready = sem("ams"), sem("ams_root"), sem("vln_ready")
        az_mm, az_ev = sem("az_mm"), sem("az_ev")
        conv_ready, dmean_mm, dsq_ready, dvar_mm, dms_root = (
            sem("conv_ready"), sem("dmean_mm"), sem("dsq_ready"), sem("dvar_mm"), sem("dms_root"))
        dlin_ready, dsig_ready, do_ready = sem("dlin_ready"), sem("dsig_ready"), sem("do_ready")
        gate_sig = sem("gate_sig")
        br_ev = sem("br_ev")
        zpad_ready = sem("zpad_ready")
        m0_done = sem("m0_done")
        yT_mm, yT_hi, yT_lo = sem("yT_mm"), sem("yT_hi"), sem("yT_lo")
        sig_ready, act_ready = sem("sig_ready"), sem("act_ready")
        aT_mm, aT_hi, aT_lo = sem("aT_mm"), sem("aT_hi"), sem("aT_lo")
        router_in, tok_hi, tok_lo, wr_hi, wr_lo = (sem("router_in"), sem("tok_hi"), sem("tok_lo"), sem("wr_hi"),
                                                   sem("wr_lo"))
        lg_mm, top_ready, wtop_ready, member_ready, rank_mm, tab_ready = (
            sem("lg_mm"), sem("top_ready"), sem("wtop_ready"), sem("member_ready"), sem("rank_mm"),
            sem("tab_ready"))
        e_sig, e_act = sem("e_sig"), sem("e_act")
        silu_ready, e_silu = sem("silu_ready"), sem("e_silu")
        wslot_ready, diff_ready = sem("wslot_ready"), sem("diff_ready")
        e_aT_mm, e_aT_hi, e_aT_lo = sem("e_aT_mm"), sem("e_aT_hi"), sem("e_aT_lo")
        pick_ready, pick_mm, pickT_ev = sem("pick_ready"), sem("pick_mm"), sem("pickT_ev")
        gat_mm, gat_hi, gat_lo = sem("gat_mm"), sem("gat_hi"), sem("gat_lo")
        y_hi, y_lo = sem("y_hi"), sem("y_lo")
        sca_mm, sca_add = sem("sca_mm"), sem("sca_add")

        class Piece:

            def __init__(self, first, i=0, per_round=0, experts=False):
                self.number = first + per_round * i
                self.first = first
                if experts:
                    j = first - MOE_BASE
                    self.slot = j % ERING
                    before = MOE_BASE // RING if self.slot < RING else 0
                    self.landed = 16 * (per_round // ERING) * i + 16 * (before + j // ERING + 1)
                    self.raw = ering[self.slot]
                    self.depth = ERING
                else:
                    self.slot = first % RING
                    self.landed = 16 * (per_round // RING) * i + 16 * (first // RING + 1)
                    self.raw = ring[self.slot]
                    self.depth = RING

            def part(self, hf):
                return (2 * self.first + hf) % 4

        def split_hi(eng, pc, n=HALF):
            eng.wait_ge(raw_in[pc.slot], pc.landed)
            for hf in range(2):
                if pc.first >= 2:
                    eng.wait_ge(w_used, 2 * pc.number + hf - 3)
                nc.scalar.copy(whi[pc.part(hf)][:, 0:n], pc.raw[:, hf * n:(hf + 1) * n]).then_inc(hi_done, 1)

        def split_lo(eng, pc, n=HALF):
            for hf in range(2):
                eng.wait_ge(hi_done, 2 * pc.number + hf + 1)
                q = pc.part(hf)
                nc.vector.tensor_tensor(wlo[q][:, 0:n], pc.raw[:, hf * n:(hf + 1) * n],
                                        whi[q][:, 0:n].bitcast(F32), ALU.subtract).then_inc(lo_done, 1)

        def w_half(eng, pc, hf, n, cols):
            eng.wait_ge(lo_done, 2 * pc.number + hf + 1)
            q = pc.part(hf)
            return (whi[q][:, 0:n].rearrange("p (k c) -> p k c", c=cols),
                    wlo[q][:, 0:n].rearrange("p (k c) -> p k c", c=cols))

        def mm3(o, sh, sl, wh, wl, start, stop):
            nc.tensor.matmul(o, sh, wh, start=start, stop=False)
            nc.tensor.matmul(o, sh, wl, start=False, stop=False)
            return nc.tensor.matmul(o, sl, wh, start=False, stop=stop)

        def mixer_pieces(l):
            b = (MIX_PIECES + 3 * FSTEPS) * l
            return [Piece(b + i) for i in range(MIX_PIECES)]

        def piece_half(s):
            return (WIDTHS[4] * 8 if s == 6 else PIECE) // 2

        def chunk_pieces(ci):
            if ci < 3:
                return [2 * ci, 2 * ci + 1]
            if ci == 3:
                return [6]
            return [7 + 2 * (ci - 4), 8 + 2 * (ci - 4)]

        def chunk_cols(ci):
            if ci < 5:
                c = CHUNK_ORDER[ci]
                return GATES + 512 * c, WIDTHS[c]
            return 512 * (ci - 5), 512

        n_chunk = 13

        block = ctx.enter_context(nc.Block())

        @block.sync
        def _(sp):
            for m in range(MT):
                sp.dma_start(x[:, m, :], a['x'][0, P * m:P * (m + 1), :]).then_inc(x_in[m], 16)

            def fetch(pc, src, k, cols):
                if pc.first >= pc.depth:
                    sp.wait_ge(lo_done, 2 * pc.number - 2 * pc.depth + 2)
                sp.dma_start(pc.raw[:, 0:k * cols].rearrange("p (k c) -> p k c", c=cols),
                             src).then_inc(raw_in[pc.slot], 16)

            def mixer_stream(l):
                pcs = mixer_pieces(l)
                w = a['w_in'][l].rearrange("(k p) n -> p k n", p=P)
                for ci in range(n_chunk):
                    c0, n = chunk_cols(ci)
                    slots = chunk_pieces(ci)
                    kk = KD // len(slots)
                    for j, s in enumerate(slots):
                        fetch(pcs[s], w[:, kk * j:kk * (j + 1), c0:c0 + n], kk, n)
                for n in range(NB):
                    fetch(pcs[25 + n], a['w_branch'][l, n].rearrange("(k p) n -> p k n", p=P), 2, D)
                wo = a['w_out'][l].rearrange("(k p) n -> p k n", p=P)
                for j in range(4):
                    fetch(pcs[29 + j], wo[:, 2 * j:2 * j + 2, :], 2, D)

            wg = a['ffn_w_gate'][0].rearrange("(k p) n -> p k n", p=P)
            wu = a['ffn_w_up'][0].rearrange("(k p) n -> p k n", p=P)
            wd = a['ffn_w_down'][0].rearrange("(s k p) n -> s p k n", p=P, k=2)

            mixer_stream(0)
            fetch(Piece(FFN_BASE), wg[:, :, 0:FSTEP], KD, FSTEP)
            fetch(Piece(FFN_BASE + 1), wu[:, :, 0:FSTEP], KD, FSTEP)

            def ffn_fetch(i, first, it, per):
                fetch(Piece(first, it, per), wg[:, :, bass.ds(i * FSTEP, FSTEP)], KD, FSTEP)
                fetch(Piece(first + 1, it, per), wu[:, :, bass.ds(i * FSTEP, FSTEP)], KD, FSTEP)
                fetch(Piece(first + 2, it, per), wd[bass.ds(i - 1, 1)].rearrange("s p k n -> (s p) k n"), 2, D)

            with sp.Fori(0, 4) as it:
                for r in range(2):
                    ffn_fetch(2 * it + 1 + r, FFN_BASE + 2 + 3 * r, it, 6)
            for i in (9, 10):
                ffn_fetch(i, FFN_BASE + 2 + 3 * (i - 1), 0, 0)
            fetch(Piece(FFN_BASE + 32), wd[10], 2, D)
            mixer_stream(1)

            eg = a['moe_w_gate'][0].rearrange("e (k p) n -> e p k n", p=P)
            eu = a['moe_w_up'][0].rearrange("e (k p) n -> e p k n", p=P)
            ed = a['moe_w_down'][0].rearrange("e (k p) n -> e p k n", p=P)

            def expert_stream(p, e):
                sp.wait_ge(lo_done, 2 * MOE_BASE)
                for j, (kind, s) in enumerate(ORDER):
                    n = ESTEPS[s]
                    pc = Piece(MOE_BASE + j, p, PASS_PIECES, experts=True)
                    if j == RING:
                        sp.wait_ge(layer_done, 2)
                    if kind == "d":
                        src = ed[bass.ds(e, 1), :, 2 * s:2 * s + n // P, :].rearrange("e p k n -> (e p) k n")
                        fetch(pc, src, n // P, D)
                    else:
                        w = eg if kind == "g" else eu
                        fetch(pc, w[bass.ds(e, 1), :, :, 256 * s:256 * s + n].rearrange("e p k n -> (e p) k n"), KD, n)

            with sp.Fori(0, NE - 1) as p:
                expert_stream(p, p)
            sp.wait_ge(tab_ready, 1)
            last_pass = sp.value_load(lasti[0:1, 0:1], min_val=NE - 1, max_val=PASSES - 2)
            with sp.Fori(NE - 1, last_pass + 1) as p:
                e = sp.value_load(eidi[0:1, bass.ds(p, 1)], min_val=0, max_val=NE - 1)
                expert_stream(p, e)
            sp.wait_ge(sca_add, 4 * last_pass + 4)
            sp.dma_start(out[0].rearrange("(m p) d -> p m d", p=P), x[:, :, :]).then_inc(out_done, 16)
            sp.wait_ge(out_done, 16)

        @block.gpsimd
        def _(pool):
            pool.dma_start(posi[:, :], a['positions'][0].rearrange("(m p) -> p m", p=P),
                           allow_slow_non_contiguous=True).then_inc(pos_in, 16)

            def load_gain(k):
                if k:
                    pool.wait_ge(gain_free, 2 * k)
                src = a['attn_norm' if k % 2 == 0 else 'ffn_norm'][k // 2:k // 2 + 1, :]
                pool.dma_start(gain[:, :], src.to_broadcast([P, D])).then_inc(gain_in, 16)

            def row(dst, src, slow=False):
                pool.dma_start(dst, src, allow_slow_non_contiguous=slow).then_inc(param_in, 16)

            def load_params(l):
                def vec(name):
                    return a[name][l:l + 1, :]
                for i, w in enumerate('qk'):
                    row(bgain[:, i, :], vec(f'b_{w}n').to_broadcast([P, HD]))
                    row(cqkgain[:, i, :], vec(f'c_{w}n').to_broadcast([P, C_QK]))
                row(cngain[:, 0:CQ], vec('c_cq_norm').to_broadcast([P, CQ]))
                row(cngain[:, CQ:CQ + CKV], vec('c_ckv_norm').to_broadcast([P, CKV]))
                row(again[:, 0, :], vec('a_ln_g').to_broadcast([P, BW]))
                row(again[:, 1, :], vec('a_ln_b').to_broadcast([P, BW]))
                row(wsr[:, :, :], a['a_ws'][l].rearrange("g t s -> t g s"))
                row(abs_[:, :], a['a_bs'][l].rearrange("g t -> t g"), slow=True)
                row(uq[:, 0, :], a['c_w_uq'][l, 0:P, :])
                row(uq[0:CQ - P, 1, :], a['c_w_uq'][l, P:CQ, :])
                row(ukv[:, :], a['c_w_ukv'][l])
                row(cwr[0:D_CONV, :], a['d_conv_w'][l])
                for i, name in enumerate(('d_conv_b', 'd_ln_g', 'd_ln_b')):
                    row(dcol[:, i, :], a[name][l].rearrange("(c p) -> p c", p=P), slow=True)

            load_gain(0)
            nc.gpsimd.memset(ident[:, :], 0.0).then_inc(pool_seq, 1)
            nc.gpsimd.memset(tri384[:, :], 0.0).then_inc(pool_seq, 1)
            nc.gpsimd.memset(upper[:, :], 1.0).then_inc(pool_seq, 1)
            nc.gpsimd.memset(upstrict[:, :], 1.0).then_inc(pool_seq, 1)
            nc.gpsimd.memset(ones[:, :], 1.0)
            nc.gpsimd.memset(mean_w[:, :], 1.0 / BW)
            nc.gpsimd.memset(eps[:, :], EPS)
            for i in range(16):
                nc.gpsimd.memset(inv[:, i:i + 1], float(np.float32(THETA) ** np.float32(-2.0 * i / 32)))
            pool.wait_ge(pool_seq, 4)
            nc.gpsimd.affine_select(out=ident[:, :], in_=ident[:, :], compare_op=ALU.not_equal, fill=1.0, base=0,
                                    pattern=[[-1, P]], channel_multiplier=1)
            for c in (0, 256):
                nc.gpsimd.affine_select(out=tri384[:, c:c + P], in_=tri384[:, c:c + P], compare_op=ALU.is_ge,
                                        fill=NEG, base=0, pattern=[[-1, P]], channel_multiplier=1)
            nc.gpsimd.affine_select(out=upper[:, :], in_=upper[:, :], compare_op=ALU.is_ge, fill=0.0, base=0,
                                    pattern=[[1, P]], channel_multiplier=-1)
            nc.gpsimd.affine_select(out=upstrict[:, :], in_=upstrict[:, :], compare_op=ALU.is_gt, fill=0.0, base=0,
                                    pattern=[[1, P]], channel_multiplier=-1).then_inc(const_ready, 1)
            load_params(0)
            pool.dma_start(wr[:, :, :], a['moe_router'][0].rearrange("(k p) e -> p k e", p=P)).then_inc(router_in, 16)
            pool.dma_start(rbias[:, :], a['moe_router_b'][0:1, :].to_broadcast([P, NE])).then_inc(router_in, 16)
            load_gain(1)
            pool.wait_ge(layer_done, 1)
            load_params(1)
            load_gain(2)
            load_gain(3)
            pool.wait_ge(layer_done, 2)
            nc.gpsimd.iota(iotai[:, :], pattern=[[1, P]], base=0, channel_multiplier=0).then_inc(iota_ready, 1)

        @block.tensor
        def _(pe):
            def transposed_h(k):
                for m in range(MT):
                    pe.wait_ge(h_ready, 2 * k + m + 1)
                    for g in range(2):
                        for j in range(4):
                            last = nc.tensor.transpose(bank[4 + 2 * m + g][:, P * j:P * (j + 1)],
                                                       hm[:, m, P * (4 * g + j):P * (4 * g + j + 1)], ident[:, :])
                        last.then_inc(hT_mm, 1)

            def prep(l):
                pe.wait_ge(param_in, 16 * N_PARAM * (l + 1))
                pe.wait_ge(hT_lo, 8 * l + 4)
                for g in range(4):
                    nc.tensor.transpose(bank[7][:, P * g:P * (g + 1)], wsr[:, g, :], ident[:, :])
                for c in range(2):
                    last = nc.tensor.transpose(bank[6][:, 32 * c:32 * c + D_CONV], cwr[0:D_CONV, P * c:P * (c + 1)],
                                               ident[0:D_CONV, 0:D_CONV])
                last.then_inc(wprep_mm, 1)

            def c_latent_T(l):
                pe.wait_ge(cn_ready, l + 1)
                pe.wait_ge(wprep_ev, l + 1)
                for m in range(MT):
                    o = P * m
                    nc.tensor.transpose(bank[4][:, o:o + P], cn[:, m, 0:P], ident[:, :])
                    nc.tensor.transpose(bank[4][:, 256 + o:256 + o + P], cn[:, m, CQ:CQ + CKV], ident[:, :])
                    last = nc.tensor.transpose(bank[5][0:CQ - P, o:o + P], cn[:, m, P:CQ], ident[:, :])
                last.then_inc(cnT_mm, 1)

            def c_up(l):
                pe.wait_ge(cnT_ev, l + 1)
                for m in range(MT):
                    t = slice(P * m, P * (m + 1))
                    nc.tensor.matmul(bank[4 + m][:, 0:384], cT[:, 0, t], uq[:, 0, :], start=True, stop=False)
                    nc.tensor.matmul(bank[4 + m][:, 0:384], cT[0:CQ - P, 2, t], uq[0:CQ - P, 1, :], start=False,
                                     stop=True)
                    last = nc.tensor.matmul(bank[6 + m][:, :], cT[:, 1, t], ukv[:, :], start=True, stop=True)
                last.then_inc(up_mm, 1)

            def c_qkT(l):
                pe.wait_ge(cqk_ready, l + 1)
                pe.wait_ge(up_ev, l + 1)
                for w, src in enumerate((ctq, kc)):
                    for hd in range(HEADS):
                        for m in range(MT):
                            b = bank[4 + 2 * w + hd // 2]
                            o = T * (hd % 2) + P * m
                            last = nc.tensor.transpose(b[0:C_QK, o:o + P], src[:, m, C_QK * hd:C_QK * (hd + 1)],
                                                       ident[:, :])
                    last.then_inc(qT_mm, 1)

            def b_qkT(l):
                pe.wait_ge(bqk_ready, l + 1)
                pe.wait_ge(o_lo[2], l + 1)
                for w in range(2):
                    for c in range(2):
                        for m in range(MT):
                            last = nc.tensor.transpose(bank[4 + w][:, T * c + P * m:T * c + P * (m + 1)],
                                                       prj[:, m, B_Q + BW * w + P * c:B_Q + BW * w + P * (c + 1)],
                                                       ident[:, :])
                    last.then_inc(qT_mm, 1)

            def scores(l, which):
                n = 2 * l + which
                pe.wait_ge(qT_evA, n + 1)
                pe.wait_ge(qT_evV, n + 1)
                if which:
                    pe.wait_ge(zpad_ready, l + 1)
                for hd in range(HEADS):
                    if which == 0:
                        q, k = qkT[0:C_QK, 0, hd, :], qkT[0:C_QK, 1, hd, :]
                    else:
                        o = HD * (hd % 2)
                        q = qkT[o:o + HD, 0, hd // 2, :]
                        k = qkT[o:o + HD, 0, 2 + hd // 2, :]
                    nc.tensor.matmul(bank[4 + hd][:, 0:P], q[:, 0:P], k[:, 0:P], start=True, stop=True)
                    nc.tensor.matmul(bank[4 + hd][:, P:384], q[:, P:T], k[:, 0:T], start=True,
                                     stop=True).then_inc(sc_mm, 1)

            def probs_T(l, which):
                n = 2 * l + which
                pe.wait_ge(pn_ready, n + 1)
                if which:
                    pe.wait_ge(az_ev, l + 1)
                for hd in range(HEADS):
                    for j in range(3):
                        last = nc.tensor.transpose(bank[4 + hd][:, P * j:P * (j + 1)],
                                                   probs[:, hd, P * j:P * (j + 1)], ident[:, :])
                    last.then_inc(pT_mm, 1)

            def values(l, which):
                n = 2 * l + which
                pe.wait_ge(pT_evA, 2 * n + 2)
                pe.wait_ge(pT_evV, 2 * n + 2)
                for hd in range(HEADS):
                    o = HD * (hd % 2)
                    c = T * (hd // 2)
                    if which == 0:
                        v = [ckv[:, m, 128 * hd + HD:128 * (hd + 1)] for m in range(MT)]
                    else:
                        v = [prj[:, m, B_V + HD * hd:B_V + HD * (hd + 1)] for m in range(MT)]
                    nc.tensor.matmul(bank[4][o:o + HD, c:c + T], v[0], pT[:, hd, 0:T], start=True, stop=False)
                    last = nc.tensor.matmul(bank[4][o:o + HD, c + P:c + T], v[1], pT[:, hd, T:384], start=False,
                                            stop=True)
                last.then_inc(o_mm[2 - which], 1)

            def d_zT(l):
                pe.wait_ge(glu_ready, l + 1)
                pe.wait_ge(pT_evV, 4 * l + 2)
                for c in range(2):
                    for m in range(MT):
                        last = nc.tensor.transpose(bank[6][:, T * c + P * m:T * c + P * (m + 1)],
                                                   dxc[:, m, P * c:P * (c + 1)], ident[:, :])
                last.then_inc(zT_mm, 1)

            def a_z(l):
                pe.wait_ge(vln_ready, l + 1)
                pe.wait_ge(sc_ev, 8 * l + 8)
                for m in range(MT):
                    for g in range(4):
                        o = BW * m + HD * g
                        last = nc.tensor.matmul(bank[4][:, o:o + HD], wsT[:, g, :],
                                                prj[:, m, A_V + HD * g:A_V + HD * (g + 1)], start=True, stop=True)
                last.then_inc(az_mm, 1)

            def a_oT(l):
                pe.wait_ge(pT_evV, 4 * l + 4)
                for c in range(2):
                    for m in range(MT):
                        last = nc.tensor.transpose(bank[6][:, T * c + P * m:T * c + P * (m + 1)],
                                                   prj[:, m, A_U + P * c:A_U + P * (c + 1)], ident[:, :])
                last.then_inc(o_mm[0], 1)

            def d_mean(l, src, ready, done, b):
                pe.wait_ge(ready, l + 1)
                for c in range(2):
                    last = nc.tensor.matmul(bank[b][:, 0:T], mean_w[:, :], src[:, c, :], start=(c == 0),
                                            stop=(c == 1))
                last.then_inc(done, 1)

            def tile_by_tile(pc, b0, tokens, start, bank_read=None):
                w = [w_half(pe, pc, hf, HALF, D) for hf in range(2)]
                for m in range(MT):
                    for c in range(2):
                        if bank_read is not None:
                            bank_read(m, c)
                        for hf in range(2):
                            sh, sl = tokens(m, hf)
                            o = slice(512 * c, 512 * (c + 1))
                            last = mm3(bank[b0 + 2 * m + c][:, :], sh, sl, w[hf][0][:, 0, o], w[hf][1][:, 0, o],
                                       start and hf == 0, hf == 1)
                            if m == 1 and c == 1:
                                last.then_inc(w_used, 1)
                    if m == 0:
                        last.then_inc(m0_done, 1)

            def mixer(l):
                pcs = mixer_pieces(l)

                def proj_piece(ci, s):
                    c0, n = chunk_cols(ci)
                    slots = chunk_pieces(ci)
                    kk = KD // len(slots)
                    k0 = kk * slots.index(s)
                    if s == slots[0] and ci >= 2:
                        pe.wait_ge(prj_ev, n_chunk * l + ci - 1)
                    b = 2 * (ci % 2)
                    for hf in range(2):
                        wh, wl = w_half(pe, pcs[s], hf, kk // 2 * n, n)
                        for j in range(kk // 2):
                            k = k0 + kk // 2 * hf + j
                            for m in range(MT):
                                t = slice(P * m, P * (m + 1))
                                last = mm3(bank[b + m][:, 0:n], hTh[:, k, t], hTl[:, k, t], wh[:, j, :],
                                           wl[:, j, :], k == 0, k == KD - 1)
                        last.then_inc(w_used, 1)

                def small(s):
                    if s == 2:
                        prep(l)
                    if s == 4:
                        c_latent_T(l)
                    if s == 5:
                        c_up(l)
                    if s == 8:
                        c_qkT(l)
                    if s == 9:
                        scores(l, 0)
                    if s == 11:
                        probs_T(l, 0)
                    if s == 12:
                        values(l, 0)
                        d_zT(l)
                    if s == 13:
                        b_qkT(l)
                    if s == 14:
                        scores(l, 1)
                    if s == 15:
                        a_z(l)
                    if s == 16:
                        probs_T(l, 1)
                    if s == 17:
                        values(l, 1)
                        a_oT(l)
                    if s == 23:
                        d_mean(l, dacc, conv_ready, dmean_mm, 7)
                    if s == 24:
                        d_mean(l, zpad[:, :, 0:T], dsq_ready, dvar_mm, 5)

                pe.wait_ge(hT_lo, 8 * l + 4)
                for ci in range(n_chunk):
                    for s in chunk_pieces(ci):
                        proj_piece(ci, s)
                        small(s)

                for n in range(NB):
                    pc = pcs[25 + n]
                    pe.wait_ge(o_lo[n], l + 1)
                    if n == 1:
                        pe.wait_ge(dms_root, l + 1)
                    if n == 0:
                        pe.wait_ge(prj_ev, n_chunk * (l + 1))
                    tile_by_tile(pc, 4 * (n % 2), lambda m, hf: (oTh[:, n, hf, P * m:P * (m + 1)],
                                                                 oTl[:, n, hf, P * m:P * (m + 1)]), True,
                                 (lambda m, c: pe.wait_ge(br_ev, 4 * (NB * l + n - 2) + 2 * m + c + 1))
                                 if n >= 2 else None)

                for m in range(MT):
                    for g in range(2):
                        pe.wait_ge(br_ev, 4 * (NB * l + 3) + 2 * m + g + 1)
                        for j in range(4):
                            last = nc.tensor.transpose(bank[4 + 2 * m + g][:, P * j:P * (j + 1)],
                                                       hm[:, m, P * (4 * g + j):P * (4 * g + j + 1)], ident[:, :])
                        last.then_inc(yT_mm, 1)
                pe.wait_ge(yT_lo, 4 * (l + 1))
                for j in range(3):
                    for hf in range(2):
                        wh, wl = w_half(pe, pcs[29 + j], hf, HALF, D)
                        k = 2 * j + hf
                        for m in range(MT):
                            t = slice(P * m, P * (m + 1))
                            for c in range(2):
                                last = mm3(bank[2 * m + c][:, :], hTh[:, k, t], hTl[:, k, t],
                                           wh[:, 0, 512 * c:512 * (c + 1)], wl[:, 0, 512 * c:512 * (c + 1)],
                                           k == 0, k == KD - 1)
                        last.then_inc(w_used, 1)

                tile_by_tile(pcs[32], 0, lambda m, hf: (hTh[:, 6 + hf, P * m:P * (m + 1)],
                                                        hTl[:, 6 + hf, P * m:P * (m + 1)]), False)

            def gate_up(pc, col, n, out_bank, st_h, st_l, tiles):
                for hf in range(2):
                    wh, wl = w_half(pe, pc, hf, 4 * n, n)
                    for j in range(4):
                        k = 4 * hf + j
                        for m in range(tiles):
                            t = slice(P * m, P * (m + 1))
                            last = mm3(out_bank(m)[:, col:col + n], st_h[:, k, t], st_l[:, k, t], wh[:, j, :],
                                       wl[:, j, :], k == 0, k == KD - 1)
                    last.then_inc(w_used, 1)

            def ffn():
                pe.wait_ge(hT_lo, 8)
                gu = lambda m: bank[4 + m]

                def step_gu(i, pg, pu, first=False):
                    if not first:
                        pe.wait_ge(act_ready, i)
                    gate_up(pg, 0, FSTEP, gu, hTh, hTl, MT)
                    gate_up(pu, FSTEP, FSTEP, gu, hTh, hTl, MT)

                def step_T(i, par):
                    pe.wait_ge(act_ready, i + 1)
                    for k in range(2):
                        for m in range(MT):
                            last = nc.tensor.transpose(bank[6 + par][:, T * k + P * m:T * k + P * (m + 1)],
                                                       act[:, m, P * k:P * (k + 1)], ident[:, :])
                    last.then_inc(aT_mm, 1)

                def step_down(i, pd, par, start, stop):
                    pe.wait_ge(aT_lo, i + 1)
                    for hf in range(2):
                        wh, wl = w_half(pe, pd, hf, HALF, D)
                        for m in range(MT):
                            t = slice(P * m, P * (m + 1))
                            for c in range(2):
                                last = mm3(bank[2 * m + c][:, :], aTh[par][:, hf, t], aTl[par][:, hf, t],
                                           wh[:, 0, 512 * c:512 * (c + 1)], wl[:, 0, 512 * c:512 * (c + 1)],
                                           start and hf == 0, stop and hf == 1)
                        last.then_inc(w_used, 1)

                step_gu(0, Piece(FFN_BASE), Piece(FFN_BASE + 1), first=True)
                step_T(0, 0)

                def body(i, par, first, it, per, start=False):
                    step_gu(i, Piece(first, it, per), Piece(first + 1, it, per))
                    step_down(i - 1, Piece(first + 2, it, per), 1 - par, start, False)
                    step_T(i, par)

                body(1, 1, FFN_BASE + 2, 0, 0, start=True)
                body(2, 0, FFN_BASE + 5, 0, 0)
                with pe.Fori(0, 3) as it:
                    for r in range(2):
                        body(2 * it + 3 + r, (3 + r) % 2, FFN_BASE + 8 + 3 * r, it, 6)
                for i in (9, 10):
                    body(i, i % 2, FFN_BASE + 2 + 3 * (i - 1), 0, 0)
                pe.wait_ge(aT_lo, 11)
                tile_by_tile(Piece(FFN_BASE + 32), 0, lambda m, hf: (aTh[0][:, hf, P * m:P * (m + 1)],
                                                                     aTl[0][:, hf, P * m:P * (m + 1)]), False)

            def router():
                pe.wait_ge(hT_lo, 16)
                pe.wait_ge(wr_lo, 1)
                for m in range(MT):
                    t = slice(P * m, P * (m + 1))
                    for k in range(KD):
                        last = mm3(bank[7][:, 8 * m:8 * m + 8], hTh[:, k, t], hTl[:, k, t], wrh[:, k, :], wrl[:, k, :],
                                   k == 0, k == KD - 1)
                last.then_inc(lg_mm, 1)
                pe.wait_ge(member_ready, 1)
                mem = [tab[:, 2 + m, 0:NE] for m in range(MT)]
                nc.tensor.matmul(bank[6][:, 0:8], upstrict[:, :], mem[0], start=True, stop=True)
                nc.tensor.matmul(bank[6][:, 8:16], upstrict[:, :], mem[1], start=True, stop=False)
                nc.tensor.matmul(bank[6][:, 8:16], ones[:, :], mem[0], start=False, stop=True)
                nc.tensor.matmul(bank[6][:, 16:24], ones[:, :], mem[0], start=True, stop=False)
                nc.tensor.matmul(bank[6][:, 16:24], ones[:, :], mem[1], start=False, stop=True).then_inc(rank_mm, 1)

            def gather(q):
                pe.wait_ge(pick_ready, q + 1)
                for k in range(KD):
                    o = bank[5 + k // 4][:, P * (k % 4):P * (k % 4 + 1)]
                    for m in range(MT):
                        c = slice(P * k, P * (k + 1))
                        nc.tensor.matmul(o, htokh[:, m, c], pick[:, m, :], start=(m == 0), stop=False)
                        last = nc.tensor.matmul(o, htokl[:, m, c], pick[:, m, :], start=False, stop=(m == MT - 1))
                    if k % 4 == 3:
                        last.then_inc(gat_mm, 1)

            def slot_rows(p):
                for m in range(MT):
                    nc.tensor.transpose(bank[7][:, P * m:P * (m + 1)], pickf[:, m, :], ident[:, :])
                for m in range(MT):
                    last = nc.tensor.matmul(bank[7][:, T:T + 1], pickf[:, m, :], wcol[:, m:m + 1], start=(m == 0),
                                            stop=(m == MT - 1))
                last.then_inc(pick_mm, 1)

            def scatter(q):
                pe.wait_ge(y_lo, 2 * q + 2)
                for m in range(MT):
                    for c in range(2):
                        o = bank[(5, 0)[m] + c][:, :]
                        r = slice(512 * c, 512 * (c + 1))
                        nc.tensor.matmul(o, pickT[:, P * m:P * (m + 1)], yh[:, r], start=True, stop=False)
                        nc.tensor.matmul(o, pickT[:, P * m:P * (m + 1)], yl[:, r], start=False,
                                         stop=True).then_inc(sca_mm, 1)

            def expert_pass(p, before=None):
                first = before is None
                pe.wait_ge(gat_lo, 2 * p + 2)

                def down(s, pc):
                    pe.wait_ge(e_aT_lo, 6 * p + s + 1)
                    if s == 0 and not first:
                        pe.wait_ge(sca_add, 4 * p)
                    nk = ESTEPS[s] // P
                    for hf in range(2):
                        wh, wl = w_half(pe, pc, hf, nk * D // 2, 512)
                        for c in range(nk):
                            k, cc = (hf, c) if nk == 2 else (0, hf)
                            last = mm3(bank[cc][:, :], aTh[s % 2][:, k, 0:P], aTl[s % 2][:, k, 0:P], wh[:, c, :],
                                       wl[:, c, :], s == 0 and k == 0, s == 5)
                        last.then_inc(w_used, 1)

                def turn(s):
                    pe.wait_ge(e_act, 6 * p + s + 1)
                    for k in range(ESTEPS[s] // P):
                        last = nc.tensor.transpose(bank[4][:, P * k:P * (k + 1)], act[:, 0, P * k:P * (k + 1)],
                                                   ident[:, :])
                    last.then_inc(e_aT_mm, 1)

                for j, (kind, s) in enumerate(ORDER):
                    pc = Piece(MOE_BASE + j, p, PASS_PIECES, experts=True)
                    n = ESTEPS[s]
                    gu = lambda m: bank[2 + s % 2]
                    if kind == "d":
                        down(s, pc)
                        if s < 5:
                            turn(s + 1)
                        continue
                    gate_up(pc, 0 if kind == "g" else n, n, gu, xgh, xgl, 1)
                    if kind == "u" and s == 0:
                        if not first:
                            scatter(before)
                        slot_rows(p)
                        turn(0)
                    if kind == "u" and s == 5:
                        gather(p + 1)

            pe.wait_ge(const_ready, 1)
            transposed_h(0)
            mixer(0)
            transposed_h(1)
            ffn()
            transposed_h(2)
            mixer(1)
            transposed_h(3)
            router()
            pe.wait_ge(tab_ready, 1)
            last_pass = pe.value_load(lasti[0:1, 0:1], min_val=NE - 1, max_val=PASSES - 2)
            gather(0)
            expert_pass(0)
            with pe.Fori(0, last_pass) as r:
                expert_pass(r + 1, before=r)
            scatter(last_pass)

        @block.scalar
        def _(act_e):
            own = [0]

            def link(ins):
                own[0] += 1
                ins.then_inc(act_seq, 1)
                act_e.wait_ge(act_seq, own[0])

            def token_norm(k):
                nc.scalar.activation(stat[:, 62:63], eps[:, 0:1], ACT.Sqrt)
                for m in range(MT):
                    if k == 0:
                        act_e.wait_ge(x_in[m], 16)
                    else:
                        act_e.wait_ge(x_new, 4 * (k - 1) + 2 * m + 2)
                    link(nc.scalar.activation(hm[:, m, :], x[:, m, :], ACT.Square, accum_out=ssum[:, m:m + 1]))
                    nc.scalar.activation(rstd[:, 0, m:m + 1], ssum[:, m:m + 1], ACT.Sqrt, bias=eps[:, 0:1],
                                         scale=1.0 / D).then_inc(rms_root, 1)
                if k:
                    norm_upper(k)

            def norm_upper(k):
                for m in range(MT):
                    for g in range(2):
                        act_e.wait_ge(hT_mm, 4 * k + 2 * m + g + 1)
                        nc.scalar.copy(hTh[:, 4 * g:4 * g + 4, P * m:P * (m + 1)],
                                       bank[4 + 2 * m + g][:, :].rearrange("p (k t) -> p k t", t=P)).then_inc(hT_hi, 1)

            def attention_exp(l, which):
                act_e.wait_ge(mx_ready, 2 * l + which + 1)
                for m in range(MT):
                    for hd in range(HEADS):
                        seg = probs[:, hd, 0:P] if m == 0 else probs[:, hd, P:384]
                        last = nc.scalar.activation(seg, seg, ACT.Exp, bias=stat[:, 4 * m + hd:4 * m + hd + 1],
                                                    accum_out=stat[:, 8 + 4 * m + hd:9 + 4 * m + hd])
                last.then_inc(ex_done, 1)

            def probs_T_ev(l, which):
                n = 2 * l + which
                for hd in range(2):
                    act_e.wait_ge(pT_mm, 4 * n + hd + 1)
                    nc.scalar.copy(pT[:, hd, :], bank[4 + hd][:, 0:384]).then_inc(pT_evA, 1)

            def o_upper(l, n, b):
                act_e.wait_ge(o_mm[n], l + 1)
                nc.scalar.copy(oTh[:, n, :, :], bank[b][:, :].rearrange("p (c t) -> p c t", t=T)).then_inc(o_hi[n], 1)

            def gate_sigmoid(l, n):
                act_e.wait_ge(prj_ev, n_chunk * l + 5 + 2 * (n + 1))
                for m in range(MT):
                    g = gates[:, m, D * n:D * (n + 1)]
                    nc.scalar.activation(g, g, ACT.Sigmoid).then_inc(gate_sig, 1)

            def mixer(l):
                pcs = mixer_pieces(l)
                last_of = {chunk_pieces(ci)[-1]: ci for ci in range(n_chunk)}

                def chunk_ev(ci):
                    c0, n = chunk_cols(ci)
                    act_e.wait_ge(w_used, 2 * pcs[chunk_pieces(ci)[-1]].number + 2)
                    for m in range(MT):
                        dst = prj[:, m, c0 - GATES:c0 - GATES + n] if ci < 5 else gates[:, m, c0:c0 + n]
                        last = nc.scalar.copy(dst, bank[2 * (ci % 2) + m][:, 0:n])
                    last.then_inc(prj_ev, 1)

                for s in range(MIX_PIECES):
                    if s + 2 < MIX_PIECES:
                        split_hi(act_e, pcs[s + 2], piece_half(s + 2))
                    elif l == 0:
                        split_hi(act_e, Piece(FFN_BASE + s + 2 - MIX_PIECES))
                    if s in last_of:
                        chunk_ev(last_of[s])
                    if s == 3:
                        act_e.wait_ge(cms, l + 1)
                        nc.scalar.activation(stat[:, 16:18], stat[:, 16:18], ACT.Sqrt, bias=eps[:, 0:1], scale=1.0 / CQ)
                        nc.scalar.activation(stat[:, 18:20], stat[:, 18:20], ACT.Sqrt, bias=eps[:, 0:1],
                                             scale=1.0 / CKV).then_inc(cms_root, 1)
                    if s == 4:
                        act_e.wait_ge(cnT_mm, l + 1)
                        nc.scalar.copy(cT[:, 0:2, :], bank[4][:, :].rearrange("p (c t) -> p c t", t=T))
                        nc.scalar.copy(cT[0:CQ - P, 2, :], bank[5][0:CQ - P, 0:T]).then_inc(cnT_ev, 1)
                    if s == 5:
                        act_e.wait_ge(up_mm, l + 1)
                        for m in range(MT):
                            nc.scalar.copy(ctq[:, m, :], bank[4 + m][:, 0:384])
                            last = nc.scalar.copy(ckv[:, m, :], bank[6 + m][:, :])
                        last.then_inc(up_ev, 1)
                    if s == 6:
                        act_e.wait_ge(qms, l + 1)
                        nc.scalar.activation(stat[:, 20:36], stat[:, 20:36], ACT.Sqrt, bias=eps[:, 0:1],
                                             scale=1.0 / C_QK).then_inc(qms_root, 1)
                    if s == 8:
                        act_e.wait_ge(ams, l + 1)
                        nc.scalar.activation(stat[:, 40:44:2], stat[:, 41:45:2], ACT.Sqrt,
                                             bias=eps[:, 0:1]).then_inc(ams_root, 1)
                        act_e.wait_ge(qT_mm, 4 * l + 1)
                        for c in range(2):
                            last = nc.scalar.copy(qkT[0:C_QK, 0, 2 * c:2 * c + 2, :],
                                                  bank[4 + c][0:C_QK, :].rearrange("p (h t) -> p h t", t=T))
                        last.then_inc(qT_evA, 1)
                    if s == 9:
                        attention_exp(l, 0)
                    if s == 10:
                        g = prj[:, :, D_G:D_G + BW]
                        nc.scalar.activation(g, g, ACT.Sigmoid).then_inc(glu_sig, 1)
                    if s == 11:
                        probs_T_ev(l, 0)
                        act_e.wait_ge(bms, l + 1)
                        nc.scalar.activation(stat[:, 20:36], stat[:, 20:36], ACT.Sqrt, bias=eps[:, 0:1],
                                             scale=1.0 / HD).then_inc(bms_root, 1)
                    if s == 12:
                        o_upper(l, 2, 4)
                        act_e.wait_ge(zT_mm, l + 1)
                        nc.scalar.copy(zpad[:, :, D_CONV - 1:D_CONV - 1 + T],
                                       bank[6][:, :].rearrange("p (c t) -> p c t", t=T)).then_inc(zpad_ready, 1)
                    if s == 13:
                        act_e.wait_ge(qT_mm, 4 * l + 3)
                        nc.scalar.copy(qkT[:, 0, 0:2, :],
                                       bank[4][:, :].rearrange("p (h t) -> p h t", t=T)).then_inc(qT_evA, 1)
                    if s == 14:
                        attention_exp(l, 1)
                    if s == 16:
                        probs_T_ev(l, 1)
                    if s == 17:
                        o_upper(l, 1, 4)
                        o_upper(l, 0, 6)
                    if s == 22:
                        gate_sigmoid(l, 0)
                        gate_sigmoid(l, 1)
                    if s == 24:
                        act_e.wait_ge(dvar_mm, l + 1)
                        nc.scalar.activation(dsd, bank[5][:, 0:T], ACT.Sqrt, bias=eps[:, 0:1]).then_inc(dms_root, 1)
                        act_e.wait_ge(dlin_ready, l + 1)
                        nc.scalar.activation(zpad[:, :, 0:T], dxc[:, :, :], ACT.Sigmoid).then_inc(dsig_ready, 1)
                        gate_sigmoid(l, 2)
                    if s == 25:
                        act_e.wait_ge(do_ready, l + 1)
                        nc.scalar.copy(oTh[:, 3, :, :], dacc[:, :, :]).then_inc(o_hi[3], 1)
                        gate_sigmoid(l, 3)
                    if s == 28:
                        for m in range(MT):
                            for g in range(2):
                                act_e.wait_ge(yT_mm, 4 * l + 2 * m + g + 1)
                                nc.scalar.copy(hTh[:, 4 * g:4 * g + 4, P * m:P * (m + 1)],
                                               bank[4 + 2 * m + g][:, :].rearrange("p (k t) -> p k t", t=P)
                                               ).then_inc(yT_hi, 1)

            def ffn():
                def sigmoid(i, pu):
                    act_e.wait_ge(w_used, 2 * pu.number + 2)
                    for m in range(MT):
                        nc.scalar.activation(sig[:, m, :], bank[4 + m][:, 0:FSTEP], ACT.Sigmoid).then_inc(sig_ready, 1)

                def turned(i, par):
                    act_e.wait_ge(aT_mm, i + 1)
                    nc.scalar.copy(aTh[par][:, :, :],
                                   bank[6 + par][:, :].rearrange("p (k t) -> p k t", t=T)).then_inc(aT_hi, 1)

                def body(i, par, first, it, per, ahead=True):
                    pu = Piece(first + 1, it, per)
                    split_hi(act_e, pu)
                    split_hi(act_e, Piece(first + 2, it, per))
                    sigmoid(i, pu)
                    if ahead:
                        split_hi(act_e, Piece(first + 3, it, per))
                    turned(i, par)

                sigmoid(0, Piece(FFN_BASE + 1))
                split_hi(act_e, Piece(FFN_BASE + 2))
                turned(0, 0)
                with act_e.Fori(0, 4) as it:
                    for r in range(2):
                        body(2 * it + 1 + r, (1 + r) % 2, FFN_BASE + 2 + 3 * r, it, 6)
                body(9, 1, FFN_BASE + 26, 0, 0)
                body(10, 0, FFN_BASE + 29, 0, 0, ahead=False)
                for j in range(3):
                    split_hi(act_e, Piece(FFN_BASE + 32 + j))

            def expert_pass(p, before=None):
                first = before is None
                def pc(j):
                    return Piece(MOE_BASE + j, p, PASS_PIECES, experts=True)

                def half(j):
                    return ESTEPS[ORDER[j][1]] * 4

                def turned(s):
                    act_e.wait_ge(e_aT_mm, 6 * p + s + 1)
                    nk = ESTEPS[s] // P
                    nc.scalar.copy(aTh[s % 2][:, 0:nk, 0:P],
                                   bank[4][:, 0:ESTEPS[s]].rearrange("p (k t) -> p k t", t=P)).then_inc(e_aT_hi, 1)

                split_hi(act_e, pc(0))
                split_hi(act_e, pc(1))
                if not first:
                    rows_upper(before)
                for j, (kind, s) in enumerate(ORDER):
                    if j + 2 < PASS_PIECES:
                        split_hi(act_e, pc(j + 2), half(j + 2))
                    if kind == "u":
                        act_e.wait_ge(w_used, 2 * pc(j).number + 2)
                        nc.scalar.activation(sig[:, 0, 0:ESTEPS[s]], bank[2 + s % 2][:, 0:ESTEPS[s]],
                                             ACT.Sigmoid).then_inc(e_sig, 1)
                    if kind == "u" and s == 0:
                        act_e.wait_ge(pick_mm, p + 1)
                        nc.scalar.copy(pickT[:, :], bank[7][:, 0:T]).then_inc(pickT_ev, 1)
                        turned(0)
                    if kind == "u" and s == 5:
                        gathered_upper(p + 1)
                    if kind == "d" and s < 5:
                        turned(s + 1)

            def gathered_upper(q):
                for g in range(2):
                    act_e.wait_ge(gat_mm, 2 * q + g + 1)
                    nc.scalar.copy(xgh[:, 4 * g:4 * g + 4, :],
                                   bank[5 + g][:, :].rearrange("p (k t) -> p k t", t=P)).then_inc(gat_hi, 1)

            def rows_upper(q):
                act_e.wait_ge(w_used, 2 * (MOE_BASE + PASS_PIECES) + 2 * PASS_PIECES * q)
                act_e.wait_ge(wslot_ready, q + 1)
                for c in range(2):
                    nc.scalar.mul(yh[:, 512 * c:512 * (c + 1)], bank[c][:, :], wslot[:, 0:1]).then_inc(y_hi, 1)

            act_e.wait_ge(const_ready, 1)
            token_norm(0)
            split_hi(act_e, Piece(0))
            split_hi(act_e, Piece(1))
            norm_upper(0)
            act_e.wait_ge(ang_ready, 2)
            nc.scalar.activation(sinT[:, :, :], sinT[:, :, :], ACT.Sin)
            nc.scalar.activation(cosT[:, :, :], cosT[:, :, :], ACT.Sin).then_inc(trig_ready, 1)
            mixer(0)
            token_norm(1)
            ffn()
            token_norm(2)
            mixer(1)
            token_norm(3)
            for m in range(MT):
                nc.scalar.copy(htokh[:, m, :], hm[:, m, :]).then_inc(tok_hi, 1)
            act_e.wait_ge(router_in, 32)
            nc.scalar.copy(wrh[:, :, :], wr[:, :, :]).then_inc(wr_hi, 1)
            act_e.wait_ge(diff_ready, 1)
            nc.scalar.activation(wtop[:, :, :], diff[:, :, :], ACT.Sigmoid).then_inc(wtop_ready, 1)
            act_e.wait_ge(tab_ready, 1)
            last_pass = act_e.value_load(lasti[0:1, 0:1], min_val=NE - 1, max_val=PASSES - 2)
            gathered_upper(0)
            expert_pass(0)
            with act_e.Fori(0, last_pass) as r:
                expert_pass(r + 1, before=r)
            rows_upper(last_pass)

        @block.vector
        def _(dve):
            own = [0]

            def link(ins):
                own[0] += 1
                ins.then_inc(dve_seq, 1)
                dve.wait_ge(dve_seq, own[0])

            V = nc.vector

            def lower_hT(k, done, hi, first):
                for m in range(MT):
                    for g in range(2):
                        dve.wait_ge(hi, first + 2 * m + g + 1)
                        o = slice(P * m, P * (m + 1))
                        V.tensor_tensor(hTl[:, 4 * g:4 * g + 4, o],
                                        bank[4 + 2 * m + g][:, :].rearrange("p (k t) -> p k t", t=P),
                                        hTh[:, 4 * g:4 * g + 4, o].bitcast(F32), ALU.subtract).then_inc(done, 1)

            def token_norm(k):
                dve.wait_ge(gain_in, 16 * (k + 1))
                for m in range(MT):
                    dve.wait_ge(rms_root, 2 * k + m + 1)
                    link(V.reciprocal(rstd[:, 1, m:m + 1], rstd[:, 0, m:m + 1]))
                    V.scalar_tensor_tensor(out=hm[:, m, :], in0=x[:, m, :], scalar=rstd[:, 1, m:m + 1], in1=gain[:, :],
                                           op0=ALU.mult, op1=ALU.mult).then_inc(h_ready, 1)
                V.engine_nop().then_inc(gain_free, 2)
                if k:
                    norm_lower(k)

            def norm_lower(k):
                lower_hT(k, hT_lo, hT_hi, 4 * k)

            def angles():
                two_pi = 2 * np.pi
                c1 = 6.28125
                c2 = float(np.float32(np.round((two_pi - c1) * 2 ** 21) / 2 ** 21))
                c3 = float(np.float32(two_pi - c1 - c2))
                magic = 1.5 * 2 ** 23
                ang, turns, r, neg = (dacc[:, 0, 32 * i:32 * (i + 1)] for i in range(4))
                link(V.tensor_copy(posf[:, :], posi[:, :]))
                for m in range(MT):
                    last = V.tensor_scalar(ang[:, 16 * m:16 * (m + 1)], inv[:, :], posf[:, m:m + 1], None, ALU.mult)
                link(last)
                link(V.tensor_scalar(turns, ang, 1.0 / two_pi, magic, ALU.mult, ALU.add))
                link(V.tensor_scalar(turns, turns, magic, None, ALU.subtract))
                link(V.scalar_tensor_tensor(out=r, in0=turns, scalar=-c1, in1=ang, op0=ALU.mult, op1=ALU.add))
                link(V.scalar_tensor_tensor(out=r, in0=turns, scalar=-c2, in1=r, op0=ALU.mult, op1=ALU.add))
                link(V.scalar_tensor_tensor(out=r, in0=turns, scalar=-c3, in1=r, op0=ALU.mult, op1=ALU.add))
                flat = sinT[:, :, :].rearrange("p m i -> p (m i)")
                V.tensor_scalar(flat, r, 3.1415925, -3.1415925, ALU.min, ALU.max).then_inc(ang_ready, 1)
                dve.wait_ge(ang_ready, 1)
                link(V.scalar_tensor_tensor(out=neg, in0=flat, scalar=-1.0, in1=flat, op0=ALU.mult, op1=ALU.max))
                V.tensor_scalar(cosT[:, :, :].rearrange("p m i -> p (m i)"), neg, -1.0, float(np.pi / 2), ALU.mult,
                                ALU.add).then_inc(ang_ready, 1)

            def rope(x1, x2, step, tmp, heads, r2):
                t = [tmp[:, i * MT * heads * r2:(i + 1) * MT * heads * r2].rearrange(
                    "p (m h r) -> p m h r", m=MT, h=heads) for i in range(4)]
                c = cosT[:, :, ::step].unsqueeze(2).to_broadcast([P, MT, heads, r2])
                s = sinT[:, :, ::step].unsqueeze(2).to_broadcast([P, MT, heads, r2])
                V.tensor_tensor(t[0], x1, c, ALU.mult)
                V.tensor_tensor(t[1], x2, s, ALU.mult)
                V.tensor_tensor(t[2], x2, c, ALU.mult)
                link(V.tensor_tensor(t[3], x1, s, ALU.mult))
                V.tensor_tensor(x1, t[0], t[1], ALU.subtract)
                link(V.tensor_tensor(x2, t[2], t[3], ALU.add))

            def prep(l):
                dve.wait_ge(wprep_mm, l + 1)
                V.tensor_tensor(wsT[:, :, :], bank[7][:, :].rearrange("p (g t) -> p g t", t=P),
                                upper[:, :].unsqueeze(1).to_broadcast([P, 4, P]), ALU.mult)
                V.memset(zpad[:, :, 0:D_CONV - 1], 0.0)
                V.tensor_copy(cw[:, :, :], bank[6][:, 0:64].rearrange("p (c j) -> p c j", c=2)[:, :, 0:D_CONV]
                              ).then_inc(wprep_ev, 1)

            def c_norm_latents(l):
                dve.wait_ge(param_in, 16 * N_PARAM * (l + 1))
                dve.wait_ge(prj_ev, n_chunk * l + 2)
                lat = prj[:, :, C_Q:C_Q + 320]
                sq = scr0[:, 0:640].rearrange("p (m c) -> p m c", m=MT)
                link(V.tensor_tensor(sq, lat, lat, ALU.mult))
                V.tensor_reduce(stat[:, 16:18], sq[:, :, 0:CQ], AX_X, ALU.add)
                V.tensor_reduce(stat[:, 18:20], sq[:, :, CQ:320], AX_X, ALU.add).then_inc(cms, 1)
                dve.wait_ge(cms_root, l + 1)
                link(V.reciprocal(stat[:, 16:20], stat[:, 16:20]))
                for m in range(MT):
                    V.scalar_tensor_tensor(out=cn[:, m, 0:CQ], in0=lat[:, m, 0:CQ], scalar=stat[:, 16 + m:17 + m],
                                           in1=cngain[:, 0:CQ], op0=ALU.mult, op1=ALU.mult)
                    last = V.scalar_tensor_tensor(out=cn[:, m, CQ:320], in0=lat[:, m, CQ:320],
                                                  scalar=stat[:, 18 + m:19 + m], in1=cngain[:, CQ:320],
                                                  op0=ALU.mult, op1=ALU.mult)
                last.then_inc(cn_ready, 1)

            def c_sum_qk(l):
                dve.wait_ge(up_ev, l + 1)
                q4 = ctq[:, :, :].rearrange("p m (h c) -> p m h c", h=HEADS)
                k4 = kc.rearrange("p m (h c) -> p m h c", h=HEADS)
                nope = ckv[:, :, :].rearrange("p m (h c) -> p m h c", h=HEADS)[:, :, :, 0:HD]
                kr = prj[:, :, C_R:C_R + CR].unsqueeze(2).to_broadcast([P, MT, HEADS, CR])
                sq = scr0[:, 0:MT * 384].rearrange("p (m h c) -> p m h c", m=MT, h=HEADS)
                V.tensor_copy(k4[:, :, :, 0:HD], nope)
                link(V.tensor_copy(k4[:, :, :, HD:C_QK], kr))
                for w, src in enumerate((q4, k4)):
                    link(V.tensor_tensor(sq, src, src, ALU.mult))
                    dst = stat[:, 20 + 8 * w:28 + 8 * w].rearrange("p (m h) -> p m h", m=MT)
                    last = V.tensor_reduce(dst, sq, AX_X, ALU.add)
                    if w == 0:
                        link(last)
                last.then_inc(qms, 1)

            def c_rotate_qk(l):
                q4 = ctq[:, :, :].rearrange("p m (h c) -> p m h c", h=HEADS)
                k4 = kc.rearrange("p m (h c) -> p m h c", h=HEADS)
                dve.wait_ge(qms_root, l + 1)
                link(V.reciprocal(stat[:, 20:36], stat[:, 20:36]))
                for w, src in enumerate((q4, k4)):
                    rs = stat[:, 20 + 8 * w:28 + 8 * w].rearrange("p (m h) -> p m h", m=MT)
                    V.tensor_tensor(src, src, rs.unsqueeze(3).to_broadcast([P, MT, HEADS, C_QK]), ALU.mult)
                link(V.engine_nop())
                if l == 0:
                    dve.wait_ge(trig_ready, 1)
                for w, src in enumerate((ctq[:, :, :], kc)):
                    src = src.rearrange("p m (h c) -> p (m h) c", h=HEADS)
                    last = V.tensor_tensor(src, src, cqkgain[:, w, :].unsqueeze(1).to_broadcast([P, MT * HEADS, C_QK]),
                                           ALU.mult)
                link(last)
                for src in (q4, k4):
                    rope(src[:, :, :, HD:HD + 16], src[:, :, :, HD + 16:C_QK], 1, scr0, HEADS, 16)
                V.engine_nop().then_inc(cqk_ready, 1)

            def b_sum_qk(l):
                qk = prj[:, :, B_Q:B_Q + 512]
                q8 = qk.rearrange("p m (h c) -> p m h c", h=8)
                sq = scr0.rearrange("p (m h c) -> p m h c", m=MT, h=8)
                link(V.tensor_tensor(sq, q8, q8, ALU.mult))
                V.tensor_reduce(stat[:, 20:36].rearrange("p (m h) -> p m h", m=MT), sq, AX_X,
                                ALU.add).then_inc(bms, 1)

            def b_rotate_qk(l):
                qk = prj[:, :, B_Q:B_Q + 512]
                q8 = qk.rearrange("p m (h c) -> p m h c", h=8)
                dve.wait_ge(bms_root, l + 1)
                link(V.reciprocal(stat[:, 20:36], stat[:, 20:36]))
                rs = stat[:, 20:36].rearrange("p (m h) -> p m h", m=MT)
                link(V.tensor_tensor(q8, q8, rs.unsqueeze(3).to_broadcast([P, MT, 8, HD]), ALU.mult))
                for m in range(MT):
                    src = qk[:, m, :].rearrange("p (w h c) -> p w h c", w=2, h=HEADS)
                    last = V.tensor_tensor(src, src, bgain[:, :, :].unsqueeze(2).to_broadcast([P, 2, HEADS, HD]),
                                           ALU.mult)
                link(last)
                rope(q8[:, :, :, 0:8], q8[:, :, :, 8:16], 2, scr1, 8, 8)
                V.engine_nop().then_inc(bqk_ready, 1)

            def softmax_start(l, which):
                scale = (C_QK if which == 0 else HD) ** -0.5
                n = 2 * l + which
                for hd in range(HEADS):
                    dve.wait_ge(sc_mm, 4 * n + hd + 1)
                    V.scalar_tensor_tensor(out=probs[:, hd, :], in0=bank[4 + hd][:, 0:384], scalar=scale,
                                           in1=tri384[:, :], op0=ALU.mult, op1=ALU.add).then_inc(sc_ev, 1)
                dve.wait_ge(sc_ev, 4 * n + 4)
                V.tensor_reduce(stat[:, 0:4], probs[:, :, 0:P], AX_X, ALU.max, negate=True)
                V.tensor_reduce(stat[:, 4:8], probs[:, :, P:384], AX_X, ALU.max, negate=True).then_inc(mx_ready, 1)

            def softmax_end(l, which):
                dve.wait_ge(ex_done, 2 * l + which + 1)
                link(V.reciprocal(stat[:, 8:16], stat[:, 8:16]))
                V.tensor_tensor(probs[:, :, 0:P], probs[:, :, 0:P],
                                stat[:, 8:12].unsqueeze(2).to_broadcast([P, HEADS, P]), ALU.mult)
                V.tensor_tensor(probs[:, :, P:384], probs[:, :, P:384],
                                stat[:, 12:16].unsqueeze(2).to_broadcast([P, HEADS, T]), ALU.mult).then_inc(pn_ready, 1)

            def probs_T_ev(l, which):
                n = 2 * l + which
                for hd in range(2, 4):
                    dve.wait_ge(pT_mm, 4 * n + hd + 1)
                    V.tensor_copy(pT[:, hd, :], bank[4 + hd][:, 0:384]).then_inc(pT_evV, 1)

            def o_lower(l, n, b):
                dve.wait_ge(o_hi[n], l + 1)
                V.tensor_tensor(oTl[:, n, :, :], bank[b][:, :].rearrange("p (c t) -> p c t", t=T),
                                oTh[:, n, :, :].bitcast(F32), ALU.subtract).then_inc(o_lo[n], 1)

            def a_norm(l):
                dve.wait_ge(prj_ev, n_chunk * l + 5)
                for m in range(MT):
                    V.bn_stats(stat[:, 46 + 6 * m:52 + 6 * m], prj[:, m, A_V:A_V + BW])
                link(V.engine_nop())
                for m in range(MT):
                    last = V.bn_aggr(stat[:, 40 + 2 * m:42 + 2 * m], stat[:, 46 + 6 * m:52 + 6 * m])
                link(last)
                V.tensor_copy(stat[:, 36:38], stat[:, 40:44:2]).then_inc(ams, 1)
                dve.wait_ge(ams_root, l + 1)
                link(V.reciprocal(stat[:, 38:40], stat[:, 40:44:2]))
                for m in range(MT):
                    v = prj[:, m, A_V:A_V + BW]
                    last = V.tensor_scalar(v, v, stat[:, 36 + m:37 + m], stat[:, 38 + m:39 + m], ALU.subtract, ALU.mult)
                link(last)
                v = prj[:, :, A_V:A_V + BW]
                link(V.tensor_tensor(v, v, again[:, 0, :].unsqueeze(1).to_broadcast([P, MT, BW]), ALU.mult))
                V.tensor_tensor(v, v, again[:, 1, :].unsqueeze(1).to_broadcast([P, MT, BW]),
                                ALU.add).then_inc(vln_ready, 1)

            def a_gate(l):
                dve.wait_ge(az_mm, l + 1)
                z = bank[4][:, :].rearrange("p (m c) -> p m c", m=MT)
                for g in range(4):
                    u = prj[:, :, A_U + HD * g:A_U + HD * (g + 1)]
                    last = V.scalar_tensor_tensor(out=u, in0=z[:, :, HD * g:HD * (g + 1)], scalar=abs_[:, g:g + 1],
                                                  in1=u, op0=ALU.add, op1=ALU.mult)
                last.then_inc(az_ev, 1)

            def glu(l):
                dve.wait_ge(glu_sig, l + 1)
                V.tensor_tensor(dxc[:, :, :], prj[:, :, D_A:D_A + BW], prj[:, :, D_G:D_G + BW],
                                ALU.mult).then_inc(glu_ready, 1)

            def conv_taps(l, first, n):
                if first == 0:
                    dve.wait_ge(zpad_ready, l + 1)
                for i in range(first, first + n):
                    j, c = i // 2, i % 2
                    if j:
                        dve.wait_ge(dve_seq, own[0] - 1)
                    z = zpad[:, c, j:j + T]
                    if j == 0:
                        ins = V.tensor_scalar(dacc[:, c, :], z, cw[:, c, 0:1], dcol[:, 0, c:c + 1], ALU.mult, ALU.add)
                    else:
                        ins = V.scalar_tensor_tensor(out=dacc[:, c, :], in0=z, scalar=cw[:, c, j:j + 1],
                                                     in1=dacc[:, c, :], op0=ALU.mult, op1=ALU.add)
                    own[0] += 1
                    ins.then_inc(dve_seq, 1)
                if first + n == 2 * D_CONV:
                    dve.wait_ge(dve_seq, own[0])
                    V.engine_nop().then_inc(conv_ready, 1)

            def d_center(l):
                dve.wait_ge(dmean_mm, l + 1)
                link(V.tensor_tensor(dxc[:, :, :], dacc[:, :, :],
                                     bank[7][:, 0:T].unsqueeze(1).to_broadcast([P, 2, T]), ALU.subtract))
                V.tensor_tensor(zpad[:, :, 0:T], dxc[:, :, :], dxc[:, :, :], ALU.mult).then_inc(dsq_ready, 1)

            def d_finish(l):
                dve.wait_ge(dms_root, l + 1)
                link(V.reciprocal(dsd, dsd))
                link(V.tensor_tensor(dxc[:, :, :], dxc[:, :, :], dsd.unsqueeze(1).to_broadcast([P, 2, T]), ALU.mult))
                for c in range(2):
                    last = V.tensor_scalar(dxc[:, c, :], dxc[:, c, :], dcol[:, 1, c:c + 1], dcol[:, 2, c:c + 1],
                                           ALU.mult, ALU.add)
                last.then_inc(dlin_ready, 1)
                dve.wait_ge(dsig_ready, l + 1)
                V.tensor_tensor(dacc[:, :, :], dxc[:, :, :], zpad[:, :, 0:T], ALU.mult).then_inc(do_ready, 1)

            def merge(l, n, pc):
                dve.wait_ge(gate_sig, 2 * (NB * l + n + 1))
                for m in range(MT):
                    if m == 0:
                        dve.wait_ge(m0_done, 6 * l + n + 1)
                    else:
                        dve.wait_ge(w_used, 2 * pc.number + 2)
                    for c in range(2):
                        g = gates[:, m, D * n + 512 * c:D * n + 512 * (c + 1)]
                        y = hm[:, m, 512 * c:512 * (c + 1)]
                        b = bank[4 * (n % 2) + 2 * m + c][:, :]
                        if n == 0:
                            V.tensor_tensor(y, g, b, ALU.mult).then_inc(br_ev, 1)
                        else:
                            link(V.tensor_tensor(g, g, b, ALU.mult))
                            V.tensor_tensor(y, y, g, ALU.add).then_inc(br_ev, 1)

            def add_to_x(pc, stage):
                for m in range(MT):
                    if m == 0:
                        dve.wait_ge(m0_done, stage)
                    else:
                        dve.wait_ge(w_used, 2 * pc.number + 2)
                    for c in range(2):
                        o = x[:, m, 512 * c:512 * (c + 1)]
                        V.tensor_tensor(o, o, bank[2 * m + c][:, :], ALU.add).then_inc(x_new, 1)

            def mixer(l):
                pcs = mixer_pieces(l)
                taps = {13: (0, 6), 14: (6, 4), 15: (10, 4), 16: (14, 6), 17: (20, 6), 18: (26, 8), 19: (34, 8),
                        20: (42, 8), 21: (50, 8), 22: (58, 4)}
                for s in range(MIX_PIECES):
                    if s == MIX_PIECES - 1:
                        add_to_x(pcs[s], 6 * l + 5)
                    if s + 2 < MIX_PIECES:
                        split_lo(dve, pcs[s + 2], piece_half(s + 2))
                    elif l == 0:
                        split_lo(dve, Piece(FFN_BASE + s + 2 - MIX_PIECES))
                    if s == 2:
                        prep(l)
                    if s == 3:
                        c_norm_latents(l)
                    if s == 6:
                        c_sum_qk(l)
                    if s == 7:
                        c_rotate_qk(l)
                    if s == 8:
                        a_norm(l)
                        dve.wait_ge(qT_mm, 4 * l + 2)
                        for c in range(2):
                            last = V.tensor_copy(qkT[0:C_QK, 1, 2 * c:2 * c + 2, :],
                                                 bank[6 + c][0:C_QK, :].rearrange("p (h t) -> p h t", t=T))
                        last.then_inc(qT_evV, 1)
                    if s == 9:
                        softmax_start(l, 0)
                    if s == 10:
                        softmax_end(l, 0)
                    if s == 11:
                        probs_T_ev(l, 0)
                        glu(l)
                        b_sum_qk(l)
                    if s == 12:
                        o_lower(l, 2, 4)
                        b_rotate_qk(l)
                    if s == 13:
                        dve.wait_ge(qT_mm, 4 * l + 4)
                        V.tensor_copy(qkT[:, 0, 2:4, :],
                                      bank[5][:, :].rearrange("p (h t) -> p h t", t=T)).then_inc(qT_evV, 1)
                    if s == 14:
                        softmax_start(l, 1)
                    if s == 15:
                        softmax_end(l, 1)
                        a_gate(l)
                    if s == 16:
                        probs_T_ev(l, 1)
                    if s == 17:
                        o_lower(l, 1, 4)
                        o_lower(l, 0, 6)
                    if s in taps:
                        conv_taps(l, *taps[s])
                    if s == 23:
                        d_center(l)
                    if s == 24:
                        d_finish(l)
                    if s == 26:
                        dve.wait_ge(o_hi[3], l + 1)
                        V.tensor_tensor(oTl[:, 3, :, :], dacc[:, :, :], oTh[:, 3, :, :].bitcast(F32),
                                        ALU.subtract).then_inc(o_lo[3], 1)
                    if 25 <= s < 29:
                        merge(l, s - 25, pcs[s])
                    if s == 28:
                        lower_hT(l, yT_lo, yT_hi, 4 * l)
                V.engine_nop().then_inc(layer_done, 1)

            def swiglu(m, b, n, e_done, e_count, out_sem):
                s = sig[:, m, 0:n]
                V.tensor_tensor(s, s, b[:, 0:n], ALU.mult).then_inc(e_done, 1)
                dve.wait_ge(e_done, e_count)
                ins = V.tensor_tensor(act[:, m, 0:n], s, b[:, n:2 * n], ALU.mult)
                if out_sem is not None:
                    ins.then_inc(out_sem, 1)

            def ffn():
                def gated(i):
                    for m in range(MT):
                        dve.wait_ge(sig_ready, 2 * i + m + 1)
                        swiglu(m, bank[4 + m], FSTEP, silu_ready, 2 * i + m + 1, act_ready if m else None)

                def turned(i, par):
                    dve.wait_ge(aT_hi, i + 1)
                    V.tensor_tensor(aTl[par][:, :, :], bank[6 + par][:, :].rearrange("p (k t) -> p k t", t=T),
                                    aTh[par][:, :, :].bitcast(F32), ALU.subtract).then_inc(aT_lo, 1)

                def body(i, par, first, it, per, ahead=True):
                    split_lo(dve, Piece(first + 1, it, per))
                    split_lo(dve, Piece(first + 2, it, per))
                    gated(i)
                    if ahead:
                        split_lo(dve, Piece(first + 3, it, per))
                    turned(i, par)

                gated(0)
                split_lo(dve, Piece(FFN_BASE + 2))
                turned(0, 0)
                with dve.Fori(0, 4) as it:
                    for r in range(2):
                        body(2 * it + 1 + r, (1 + r) % 2, FFN_BASE + 2 + 3 * r, it, 6)
                body(9, 1, FFN_BASE + 26, 0, 0)
                body(10, 0, FFN_BASE + 29, 0, 0, ahead=False)
                split_lo(dve, Piece(FFN_BASE + 32))
                split_lo(dve, Piece(FFN_BASE + 33))
                add_to_x(Piece(FFN_BASE + 32), 6)
                split_lo(dve, Piece(FFN_BASE + 34))

            def router():
                dve.wait_ge(iota_ready, 1)
                V.tensor_copy(iotaf[:, :], iotai[:, :])
                V.memset(tab[:, :, :], 0.0)
                dve.wait_ge(wr_hi, 1)
                V.tensor_tensor(wrl[:, :, :], wr[:, :, :], wrh[:, :, :].bitcast(F32), ALU.subtract).then_inc(wr_lo, 1)
                for m in range(MT):
                    dve.wait_ge(tok_hi, m + 1)
                    V.tensor_tensor(htokl[:, m, :], hm[:, m, :], htokh[:, m, :].bitcast(F32),
                                    ALU.subtract).then_inc(tok_lo, 1)
                dve.wait_ge(lg_mm, 1)
                link(V.tensor_tensor(lg[:, :, :], bank[7][:, 0:16].rearrange("p (m e) -> p m e", m=MT),
                                     rbias[:, :].unsqueeze(1).to_broadcast([P, MT, NE]), ALU.add))
                for m in range(MT):
                    last = V.max(top8[:, m, :], lg[:, m, :])
                link(last)
                for s in range(2):
                    last = V.tensor_tensor(diff[:, :, s:s + 1], top8[:, :, s:s + 1], top8[:, :, 1 - s:2 - s],
                                           ALU.subtract)
                last.then_inc(diff_ready, 1)
                for m in range(MT):
                    last = V.max_index(idx8[:, m, :], top8[:, m, :], lg[:, m, :])
                link(last)
                link(V.tensor_copy(idxf[:, :, :], idx8[:, :, 0:2]))
                for s in range(2):
                    for m in range(MT):
                        last = V.tensor_scalar(hot[:, s, m, :], iotaf[:, 0:NE], idxf[:, m, s:s + 1], None, ALU.is_equal)
                link(last)
                V.tensor_tensor(tab[:, 2:4, 0:NE], hot[:, 0, :, :], hot[:, 1, :, :], ALU.add).then_inc(member_ready, 1)
                dve.wait_ge(member_ready, 1)
                dve.wait_ge(wtop_ready, 1)
                for m in range(MT):
                    last = V.tensor_scalar(hot[:, 0, m, :], hot[:, 0, m, :], wtop[:, m, 0:1], None, ALU.mult)
                link(last)
                for m in range(MT):
                    V.scalar_tensor_tensor(out=tab[:, 4 + m, 0:NE], in0=hot[:, 1, m, :], scalar=wtop[:, m, 1:2],
                                           in1=hot[:, 0, m, :], op0=ALU.mult, op1=ALU.add)
                dve.wait_ge(rank_mm, 1)
                V.tensor_copy(tab[:, 0:2, 0:NE], bank[6][:, 0:16].rearrange("p (m e) -> p m e", m=MT))
                V.tensor_scalar(over[:, :], bank[6][:, 16:24], float(SLOTS), None, ALU.is_gt)
                V.memset(oidx[:, 0:1], 0.0)
                link(V.tensor_copy(eidf[:, :], iotaf[:, 0:PASSES]))
                for e in range(1, NE):
                    link(V.tensor_tensor(oidx[:, e:e + 1], oidx[:, e - 1:e], over[:, e - 1:e], ALU.add))
                link(V.tensor_tensor(lastf[:, :], oidx[:, NE - 1:NE], over[:, NE - 1:NE], ALU.add))
                link(V.tensor_scalar(lastf[:, :], lastf[:, :], float(NE - 1), None, ALU.add))
                V.tensor_copy(lasti[:, :], lastf[:, :])
                for o in range(3):
                    col = NE + o
                    link(V.scalar_tensor_tensor(out=sel[:, :], in0=oidx[:, :], scalar=float(o), in1=over[:, :],
                                                op0=ALU.is_equal, op1=ALU.mult))
                    link(V.tensor_tensor(prod[:, :, :], tab[:, :, 0:NE], sel[:, :].unsqueeze(1).to_broadcast([P, 6, NE]),
                                         ALU.mult))
                    link(V.tensor_reduce(tab[:, :, col:col + 1], prod[:, :, :], AX_X, ALU.add))
                    link(V.tensor_tensor(prod[:, 0, :], iotaf[:, 0:NE], sel[:, :], ALU.mult))
                    link(V.tensor_reduce(eidf[:, col:col + 1], prod[:, 0, :], AX_X, ALU.add))
                V.tensor_scalar(tab[:, 0:2, NE:NE + 3], tab[:, 0:2, NE:NE + 3], float(SLOTS), None, ALU.subtract)
                link(V.tensor_copy(eidi[:, :], eidf[:, :]))
                V.engine_nop().then_inc(tab_ready, 1)

            def expert_pass(p, before=None):
                first = before is None
                def pc(j):
                    return Piece(MOE_BASE + j, p, PASS_PIECES, experts=True)

                def half(j):
                    return ESTEPS[ORDER[j][1]] * 4

                def turned(s):
                    dve.wait_ge(e_aT_hi, 6 * p + s + 1)
                    nk = ESTEPS[s] // P
                    V.tensor_tensor(aTl[s % 2][:, 0:nk, 0:P], bank[4][:, 0:ESTEPS[s]].rearrange("p (k t) -> p k t", t=P),
                                    aTh[s % 2][:, 0:nk, 0:P].bitcast(F32), ALU.subtract).then_inc(e_aT_lo, 1)

                split_lo(dve, pc(0))
                split_lo(dve, pc(1))
                if not first:
                    rows_lower(before)
                for j, (kind, s) in enumerate(ORDER):
                    if j + 2 < PASS_PIECES:
                        split_lo(dve, pc(j + 2), half(j + 2))
                    if kind == "u":
                        dve.wait_ge(e_sig, 6 * p + s + 1)
                        swiglu(0, bank[2 + s % 2], ESTEPS[s], e_silu, 6 * p + s + 1, e_act)
                    if kind == "u" and s == 0:
                        turned(0)
                    if j == 2:
                        if not first:
                            scattered(before)
                        dve.wait_ge(pickT_ev, p + 1)
                        V.tensor_copy(wslot[:, :], bank[7][:, T:T + 1]).then_inc(wslot_ready, 1)
                    if j == 9:
                        pick_slots(p + 1)
                    if kind == "u" and s == 5:
                        gathered_lower(p + 1)
                    if kind == "d" and s < 5:
                        turned(s + 1)

            def pick_slots(q):
                for m in range(MT):
                    rank = tab[:, m, bass.ds(q, 1)]
                    member = tab[:, 2 + m, bass.ds(q, 1)]
                    V.tensor_scalar(pick[:, m, :], iotaf[:, :], rank, member, ALU.is_equal, ALU.mult)
                    V.tensor_scalar(pickf[:, m, :], iotaf[:, :], rank, member, ALU.is_equal, ALU.mult)
                    last = V.tensor_copy(wcol[:, m:m + 1], tab[:, 4 + m, bass.ds(q, 1)])
                last.then_inc(pick_ready, 1)

            def gathered_lower(q):
                for g in range(2):
                    dve.wait_ge(gat_hi, 2 * q + g + 1)
                    V.tensor_tensor(xgl[:, 4 * g:4 * g + 4, :], bank[5 + g][:, :].rearrange("p (k t) -> p k t", t=P),
                                    xgh[:, 4 * g:4 * g + 4, :].bitcast(F32), ALU.subtract).then_inc(gat_lo, 1)

            def rows_lower(q):
                for c in range(2):
                    dve.wait_ge(y_hi, 2 * q + c + 1)
                    o = slice(512 * c, 512 * (c + 1))
                    V.scalar_tensor_tensor(out=yl[:, o], in0=bank[c][:, :], scalar=wslot[:, 0:1],
                                           in1=yh[:, o].bitcast(F32), op0=ALU.mult, op1=ALU.subtract).then_inc(y_lo, 1)

            def scattered(q):
                for m in range(MT):
                    for c in range(2):
                        dve.wait_ge(sca_mm, 4 * q + 2 * m + c + 1)
                        o = x[:, m, 512 * c:512 * (c + 1)]
                        V.tensor_tensor(o, o, bank[(5, 0)[m] + c][:, :], ALU.add).then_inc(sca_add, 1)

            dve.wait_ge(const_ready, 1)
            dve.wait_ge(pos_in, 16)
            angles()
            token_norm(0)
            split_lo(dve, Piece(0))
            split_lo(dve, Piece(1))
            norm_lower(0)
            mixer(0)
            token_norm(1)
            ffn()
            token_norm(2)
            mixer(1)
            token_norm(3)
            router()
            last_pass = dve.value_load(lasti[0:1, 0:1], min_val=NE - 1, max_val=PASSES - 2)
            pick_slots(0)
            gathered_lower(0)
            expert_pass(0)
            with dve.Fori(0, last_pass) as r:
                expert_pass(r + 1, before=r)
            rows_lower(last_pass)
            scattered(last_pass)


def kernel(**inputs):
    import concourse.bacc as bacc
    from concourse.bass_utils import run_bass_kernel_spmd

    nc = bacc.Bacc("TRN2", target_bir_lowering=False, num_devices=1)
    arrays, aps = {}, {}
    for name in INPUTS:
        v = np.ascontiguousarray(inputs[name])
        arrays[f"in_{name}"] = v
        aps[name] = nc.dram_tensor(f"in_{name}", v.shape, mybir.dt.from_np(v.dtype), kind="ExternalInput").ap()
    out = nc.dram_tensor("out_x", (1, T, D), F32, kind="ExternalOutput").ap()
    build_trunk(nc, aps, out)
    r = run_bass_kernel_spmd(nc, [arrays], core_ids=[0])
    return r.results[0]["out_x"]
```

```python
from contextlib import ExitStack

import numpy as np
import concourse.bass as bass
from concourse import mybir

F32 = mybir.dt.float32
F32R = mybir.dt.float32r
I32 = mybir.dt.int32
U32 = mybir.dt.uint32
ALU = mybir.AluOpType
ACT = mybir.ActivationFunctionType
AX_X = mybir.AxisListType.X

P = 128
D = 1024
T = 256
MT = T // P
KD = D // P
DEPTH = 2
NB = 4
BW = 256
HEADS = 4
HD = 64
B_ROT = 16
CQ, CKV, CR = 192, 128, 32
C_QK = HD + CR
D_CONV = 31
FFN = 2816
NE = 8
EDIM = 1408
GATES = NB * D
REST = 2 * BW + 3 * BW + (CQ + CKV + CR) + 2 * BW
EPS = 1e-6
NEG = -1e30
THETA = 500000.0
A_U, A_V = 0, BW
B_Q, B_K, B_V = 2 * BW, 3 * BW, 4 * BW
C_Q = 5 * BW
C_R = C_Q + CQ + CKV
D_A = C_R + CR
D_G = D_A + BW

PIECE = 2048
HALF = PIECE // 2
RING = 3
ERING = 6
CHUNK_ORDER = [2, 3, 1, 4, 0]
WIDTHS = [min(512, REST - 512 * c) for c in range(5)]
MIX_PIECES = 33
FSTEP = 256
FSTEPS = FFN // FSTEP
FFN_BASE = MIX_PIECES
MOE_BASE = 2 * MIX_PIECES + 3 * FSTEPS
ESTEPS = [256] * 5 + [128]
PASS_PIECES = 18
SLOTS = 128
PASSES = 12

ORDER = [("g", 0), ("u", 0)]
for _s in range(1, 6):
    ORDER += [("g", _s), ("u", _s), ("d", _s - 1)]
ORDER += [("d", 5)]
PAIRED = [j for j, (_k, _s) in enumerate(ORDER) if _s == 5 and _k != "d"]

INPUTS = ['x', 'positions', 'attn_norm', 'ffn_norm', 'w_in', 'a_ln_g', 'a_ln_b', 'a_ws', 'a_bs', 'b_qn', 'b_kn',
          'c_cq_norm', 'c_ckv_norm', 'c_w_uq', 'c_w_ukv', 'c_qn', 'c_kn', 'd_conv_w', 'd_conv_b', 'd_ln_g',
          'd_ln_b', 'w_branch', 'w_out', 'ffn_w_gate', 'ffn_w_up', 'ffn_w_down', 'moe_router', 'moe_router_b',
          'moe_w_gate', 'moe_w_up', 'moe_w_down']

N_PARAM = 17


def build_trunk(nc, a, out):
    with ExitStack() as ctx:
        base = (nc.sbuf_base + 63) // 64 * 64
        top = [base]

        def place(name, shape, dt=F32):
            n = 4 * int(np.prod(shape[1:]))
            t = nc.alloc_sbuf_tensor_at(name, shape, dt, offset=top[0])
            top[0] += (n + 31) // 32 * 32
            return t

        x = place("x", [P, MT, D])
        h = place("h", [P, MT * D])
        hTh = place("hTh", [P, KD, T], F32R)
        hTl = place("hTl", [P, KD, T], F32R)
        ring = [place(f"ring{i}", [P, PIECE]) for i in range(RING)]
        whi = [place(f"whi{i}", [P, HALF], F32R) for i in range(4)]
        wlo = [place(f"wlo{i}", [P, HALF], F32R) for i in range(4)]
        gain = place("gain", [P, D])
        ident = place("ident", [P, P])
        tri384 = place("tri384", [P, 384])
        upper = place("upper", [P, P])
        upstrict = place("upstrict", [P, P])
        ones = place("ones", [P, P])
        mean_w = place("mean_w", [P, P])
        eps = place("eps", [P, 1])
        wr = place("wr", [P, KD, NE])
        rbias = place("rbias", [P, NE])
        wrh = place("wrh", [P, KD, NE], F32R)
        wrl = place("wrl", [P, KD, NE], F32R)
        tab = place("tab", [P, 6, PASSES])
        iotai = place("iotai", [P, P], I32)
        iotaf = place("iotaf", [P, P])
        before_e = place("before_e", [P, NE, NE])
        inv = place("inv", [P, 16])
        cosT = place("cosT", [P, MT, 16])
        sinT = place("sinT", [P, MT, 16])
        posi = place("posi", [P, MT], I32)
        posf = place("posf", [P, MT])
        ssum = place("ssum", [P, MT])
        rstd = place("rstd", [P, 2, MT])
        stat = place("stat", [P, 64])

        shared = top[0]
        gates = place("gates", [P, MT, GATES])
        prj = place("prj", [P, MT, REST])
        ctq = place("ctq", [P, MT, HEADS * C_QK])
        ckv = place("ckv", [P, MT, 512])
        qkT = place("qkT", [P, 2, HEADS, T])
        oTh = place("oTh", [P, NB, 2, T], F32R)
        oTl = place("oTl", [P, NB, 2, T], F32R)
        zpad = place("zpad", [P, 2, D_CONV - 1 + T])
        dacc = place("dacc", [P, 2, T])
        dxc = place("dxc", [P, 2, T])
        pT = place("pT", [P, HEADS, 384])
        wsT = place("wsT", [P, 4, P])
        cw = place("cw", [P, 2, D_CONV])
        uq = place("uq", [P, 2, HEADS * C_QK])
        ukv = place("ukv", [P, 512])
        wsr = place("wsr", [P, 4, P])
        cwr = place("cwr", [P, BW])
        bgain = place("bgain", [P, 2, HD])
        cqkgain = place("cqkgain", [P, 2, C_QK])
        cngain = place("cngain", [P, CQ + CKV])
        again = place("again", [P, 2, BW])
        dcol = place("dcol", [P, 3, 2])
        abs_ = place("abs_", [P, 4])
        end = top[0]

        top[0] = shared
        sig = place("sig", [P, MT, FSTEP])
        act = place("act", [P, MT, FSTEP])
        aTh = [place(f"aTh{i}", [P, 2, T], F32R) for i in range(2)]
        aTl = [place(f"aTl{i}", [P, 2, T], F32R) for i in range(2)]
        ering = ring + [place(f"ring{i}", [P, PIECE]) for i in range(RING, ERING)]
        htokh = place("htokh", [P, MT, D], F32R)
        htokl = place("htokl", [P, MT, D], F32R)
        xgh = place("xgh", [P, KD, P], F32R)
        xgl = place("xgl", [P, KD, P], F32R)
        yh = place("yh", [P, D], F32R)
        yl = place("yl", [P, D], F32R)
        pick = place("pick", [P, MT, P], F32R)
        pickf = place("pickf", [P, MT, P])
        pickT = place("pickT", [P, T], F32R)
        wcol = place("wcol", [P, MT])
        wslot = place("wslot", [P, 1])
        lg = place("lg", [P, MT, NE])
        lgT = place("lgT", [P, T])
        top8 = place("top8", [P, MT, 8])
        idx8 = place("idx8", [P, MT, 8], U32)
        idxf = place("idxf", [P, MT, 2])
        wtop = place("wtop", [P, MT, 2])
        diff = place("diff", [P, MT, 2])
        hot = place("hot", [P, 2, MT, NE])
        prod = place("prod", [P, 3, 6, NE])
        prefix = place("prefix", [P, NE, NE])
        cnt = place("cnt", [P, NE])
        over = place("over", [P, NE])
        oidx = place("oidx", [P, NE])
        sel = place("sel", [P, 3, NE])
        eprod = place("eprod", [P, 3, NE])
        eidf = place("eidf", [P, PASSES])
        eidi = place("eidi", [P, PASSES], I32)
        lastf = place("lastf", [P, 1])
        lasti = place("lasti", [P, 1], I32)
        squares = place("squares", [P, MT, D])
        top[0] = max(end, top[0])
        assert top[0] <= nc.sbuf_usable_end, (top[0], nc.sbuf_usable_end)

        hm = h[:, :].rearrange("p (m d) -> p m d", m=MT)
        scr0, scr1 = h[:, 0:D], h[:, D:2 * D]
        probs = h[:, 0:HEADS * 384].rearrange("p (h k) -> p h k", h=HEADS)
        cT = pT[:, 0:2, :].rearrange("p h k -> p (h k)").rearrange("p (c t) -> p c t", t=T)
        dsd = pT[:, 3, 0:T]
        cn = scr1[:, 0:MT * 320].rearrange("p (m c) -> p m c", m=MT)
        kc = scr1[:, 0:MT * HEADS * C_QK].rearrange("p (m c) -> p m c", m=MT)

        bank = [ctx.enter_context(nc.psum_tensor(f"bank{i}", [P, 512], F32)) for i in range(8)]

        def sem(name):
            return ctx.enter_context(nc.semaphore(name))

        x_in = [sem(f"x_in{m}") for m in range(MT)]
        pos_in, iota_ready = sem("pos_in"), sem("iota_ready")
        out_done = sem("out_done")
        raw_in = [sem(f"raw_in{i}") for i in range(ERING)]
        hi_done, lo_done, w_used = sem("hi_done"), sem("lo_done"), sem("w_used")
        const_ready = sem("const_ready")
        pool_seq, dve_seq, act_seq = sem("pool_seq"), sem("dve_seq"), sem("act_seq")
        gain_in, gain_free = sem("gain_in"), sem("gain_free")
        param_in = sem("param_in")
        layer_done = sem("layer_done")
        x_new = sem("x_new")
        rms_root, rstd_ready, h_ready = sem("rms_root"), sem("rstd_ready"), sem("h_ready")
        hT_mm, hT_hi, hT_lo = sem("hT_mm"), sem("hT_hi"), sem("hT_lo")
        prj_ev = sem("prj_ev")
        wprep_mm, wprep_ev = sem("wprep_mm"), sem("wprep_ev")
        ang_ready, trig_ready = sem("ang_ready"), sem("trig_ready")
        cms, cms_root, cn_ready = sem("cms"), sem("cms_root"), sem("cn_ready")
        cnT_mm, cnT_ev = sem("cnT_mm"), sem("cnT_ev")
        up_mm, up_ev = sem("up_mm"), sem("up_ev")
        qms, qms_root, cqk_ready = sem("qms"), sem("qms_root"), sem("cqk_ready")
        bms, bms_root, bqk_ready = sem("bms"), sem("bms_root"), sem("bqk_ready")
        qT_mm, qT_evA, qT_evV = sem("qT_mm"), sem("qT_evA"), sem("qT_evV")
        sc_mm, sc_ev, mx_ready, ex_done, pn_ready = (sem("sc_mm"), sem("sc_ev"), sem("mx_ready"), sem("ex_done"),
                                                     sem("pn_ready"))
        pT_mm, pT_evA, pT_evV = sem("pT_mm"), sem("pT_evA"), sem("pT_evV")
        o_mm = [sem(f"o_mm{n}") for n in range(NB)]
        o_hi = [sem(f"o_hi{n}") for n in range(NB)]
        o_lo = [sem(f"o_lo{n}") for n in range(NB)]
        glu_sig, glu_ready, zT_mm = sem("glu_sig"), sem("glu_ready"), sem("zT_mm")
        ams, ams_root, vln_ready = sem("ams"), sem("ams_root"), sem("vln_ready")
        az_mm, az_ev = sem("az_mm"), sem("az_ev")
        conv_ready, dmean_mm, dsq_ready, dvar_mm, dms_root = (
            sem("conv_ready"), sem("dmean_mm"), sem("dsq_ready"), sem("dvar_mm"), sem("dms_root"))
        dlin_ready, dsig_ready, do_ready = sem("dlin_ready"), sem("dsig_ready"), sem("do_ready")
        gate_sig = sem("gate_sig")
        br_ev = sem("br_ev")
        zpad_ready = sem("zpad_ready")
        m0_done = sem("m0_done")
        yT_mm, yT_hi, yT_lo = sem("yT_mm"), sem("yT_hi"), sem("yT_lo")
        sig_ready, act_ready = sem("sig_ready"), sem("act_ready")
        aT_mm, aT_hi, aT_lo = sem("aT_mm"), sem("aT_hi"), sem("aT_lo")
        router_in, tok_hi, tok_lo, wr_hi, wr_lo = (sem("router_in"), sem("tok_hi"), sem("tok_lo"), sem("wr_hi"),
                                                   sem("wr_lo"))
        lg_mm, lgT_ev, lgT_mm, wtop_ready, member_ready, rank_mm, tab_ready = (
            sem("lg_mm"), sem("lgT_ev"), sem("lgT_mm"), sem("wtop_ready"), sem("member_ready"), sem("rank_mm"),
            sem("tab_ready"))
        e_sig, e_act = sem("e_sig"), sem("e_act")
        silu_ready, e_silu = sem("silu_ready"), sem("e_silu")
        wslot_ready, diff_ready = sem("wslot_ready"), sem("diff_ready")
        e_aT_mm, e_aT_hi, e_aT_lo = sem("e_aT_mm"), sem("e_aT_hi"), sem("e_aT_lo")
        pick_ready, pick_mm, pickT_ev = sem("pick_ready"), sem("pick_mm"), sem("pickT_ev")
        gat_mm, gat_hi, gat_lo = sem("gat_mm"), sem("gat_hi"), sem("gat_lo")
        y_hi, y_lo = sem("y_hi"), sem("y_lo")
        sca_mm, sca_add = sem("sca_mm"), sem("sca_add")

        class Piece:

            def __init__(self, first, i=0, per_round=0, experts=False):
                self.number = first + per_round * i
                self.first = first
                if experts:
                    j = first - MOE_BASE
                    self.slot = j % ERING
                    before = MOE_BASE // RING if self.slot < RING else 0
                    paired = [q for q in PAIRED if q % ERING == self.slot]
                    extra = 1 if paired and j >= paired[0] else 0
                    self.landed = (16 * (PASS_PIECES // ERING + len(paired)) * i
                                   + 16 * (before + j // ERING + 1 + extra))
                    self.raw = ering[self.slot]
                    self.depth = ERING
                else:
                    self.slot = first % RING
                    self.landed = 16 * (per_round // RING) * i + 16 * (first // RING + 1)
                    self.raw = ring[self.slot]
                    self.depth = RING

            def part(self, hf):
                return (2 * self.first + hf) % 4

        def split_hi(eng, pc, n=HALF):
            eng.wait_ge(raw_in[pc.slot], pc.landed)
            for hf in range(2):
                if pc.first >= 2:
                    eng.wait_ge(w_used, 2 * pc.number + hf - 3)
                nc.scalar.copy(whi[pc.part(hf)][:, 0:n], pc.raw[:, hf * n:(hf + 1) * n]).then_inc(hi_done, 1)

        def split_lo(eng, pc, n=HALF):
            for hf in range(2):
                eng.wait_ge(hi_done, 2 * pc.number + hf + 1)
                q = pc.part(hf)
                nc.vector.tensor_tensor(wlo[q][:, 0:n], pc.raw[:, hf * n:(hf + 1) * n],
                                        whi[q][:, 0:n].bitcast(F32), ALU.subtract).then_inc(lo_done, 1)

        def w_half(eng, pc, hf, n, cols):
            eng.wait_ge(lo_done, 2 * pc.number + hf + 1)
            q = pc.part(hf)
            return (whi[q][:, 0:n].rearrange("p (k c) -> p k c", c=cols),
                    wlo[q][:, 0:n].rearrange("p (k c) -> p k c", c=cols))

        def mm3(o, sh, sl, wh, wl, start, stop):
            nc.tensor.matmul(o, sh, wh, start=start, stop=False)
            nc.tensor.matmul(o, sh, wl, start=False, stop=False)
            return nc.tensor.matmul(o, sl, wh, start=False, stop=stop)

        def mixer_pieces(l):
            b = (MIX_PIECES + 3 * FSTEPS) * l
            return [Piece(b + i) for i in range(MIX_PIECES)]

        def after_mixer(l, j):
            return Piece(FFN_BASE + j) if l == 0 else Piece(MOE_BASE + j, 0, PASS_PIECES, experts=True)

        def piece_half(s):
            return (WIDTHS[4] * 8 if s == 6 else PIECE) // 2

        def chunk_pieces(ci):
            if ci < 3:
                return [2 * ci, 2 * ci + 1]
            if ci == 3:
                return [6]
            return [7 + 2 * (ci - 4), 8 + 2 * (ci - 4)]

        def chunk_cols(ci):
            if ci < 5:
                c = CHUNK_ORDER[ci]
                return GATES + 512 * c, WIDTHS[c]
            return 512 * (ci - 5), 512

        n_chunk = 13

        block = ctx.enter_context(nc.Block())

        @block.sync
        def _(sp):
            for m in range(MT):
                sp.dma_start(x[:, m, :], a['x'][0, P * m:P * (m + 1), :]).then_inc(x_in[m], 16)

            def fetch(pc, src, k, cols):
                if pc.first >= pc.depth:
                    sp.wait_ge(lo_done, 2 * pc.number - 2 * pc.depth + 2)
                dst = pc.raw[:, 0:k * cols].rearrange("p (k c) -> p k c", c=cols)
                if len(src.shape) == 4:
                    dst = pc.raw[:, 0:k * cols].rearrange("p (h k c) -> p h k c", h=2, c=cols)
                sp.dma_start(dst, src).then_inc(raw_in[pc.slot], 16)

            def mixer_stream(l):
                pcs = mixer_pieces(l)
                w = a['w_in'][l].rearrange("(k p) n -> p k n", p=P)
                for ci in range(n_chunk):
                    c0, n = chunk_cols(ci)
                    slots = chunk_pieces(ci)
                    kk = KD // len(slots)
                    for j, s in enumerate(slots):
                        fetch(pcs[s], w[:, kk * j:kk * (j + 1), c0:c0 + n], kk, n)
                for n in range(NB):
                    fetch(pcs[25 + n], a['w_branch'][l, n].rearrange("(k p) (c n) -> p c k n", p=P, n=512), 4, 512)
                wo = a['w_out'][l].rearrange("(k p) n -> p k n", p=P)
                for j in range(4):
                    fetch(pcs[29 + j], wo[:, 2 * j:2 * j + 2, :], 2, D)

            wg = a['ffn_w_gate'][0].rearrange("(k p) n -> p k n", p=P)
            wu = a['ffn_w_up'][0].rearrange("(k p) n -> p k n", p=P)
            wd = a['ffn_w_down'][0].rearrange("(s k p) n -> s p k n", p=P, k=2)

            mixer_stream(0)
            fetch(Piece(FFN_BASE), wg[:, :, 0:FSTEP], KD, FSTEP)
            fetch(Piece(FFN_BASE + 1), wu[:, :, 0:FSTEP], KD, FSTEP)

            def ffn_fetch(i, first, it, per):
                fetch(Piece(first, it, per), wg[:, :, bass.ds(i * FSTEP, FSTEP)], KD, FSTEP)
                fetch(Piece(first + 1, it, per), wu[:, :, bass.ds(i * FSTEP, FSTEP)], KD, FSTEP)
                fetch(Piece(first + 2, it, per), wd[bass.ds(i - 1, 1)].rearrange("s p k n -> (s p) k n"), 2, D)

            with sp.Fori(0, 4) as it:
                for r in range(2):
                    ffn_fetch(2 * it + 1 + r, FFN_BASE + 2 + 3 * r, it, 6)
            for i in (9, 10):
                ffn_fetch(i, FFN_BASE + 2 + 3 * (i - 1), 0, 0)
            fetch(Piece(FFN_BASE + 32), wd[10], 2, D)
            mixer_stream(1)

            eg = a['moe_w_gate'][0].rearrange("e (k p) n -> e p k n", p=P)
            eu = a['moe_w_up'][0].rearrange("e (k p) n -> e p k n", p=P)
            ed = a['moe_w_down'][0].rearrange("e (k p) n -> e p k n", p=P)

            def expert_stream(p, e):
                sp.wait_ge(lo_done, 2 * MOE_BASE)
                for j, (kind, s) in enumerate(ORDER):
                    n = ESTEPS[s]
                    pc = Piece(MOE_BASE + j, p, PASS_PIECES, experts=True)
                    if j == RING:
                        sp.wait_ge(layer_done, 2)
                    if kind == "d":
                        src = ed[bass.ds(e, 1), :, 2 * s:2 * s + n // P, :].rearrange("e p k n -> (e p) k n")
                        fetch(pc, src, n // P, D)
                    elif s == 5:
                        sp.wait_ge(lo_done, 2 * pc.number - 2 * pc.depth + 2)
                        k0 = 0 if kind == "g" else KD // 2
                        for i, w in enumerate((eg, eu)):
                            src = w[bass.ds(e, 1), :, k0:k0 + KD // 2, 256 * s:256 * s + n]
                            sp.dma_start(pc.raw[:, 0:KD * n].rearrange("p (k c) -> p k c", c=2 * n)[:, :, n * i:n * i + n],
                                         src.rearrange("e p k n -> (e p) k n")).then_inc(raw_in[pc.slot], 16)
                    else:
                        w = eg if kind == "g" else eu
                        fetch(pc, w[bass.ds(e, 1), :, :, 256 * s:256 * s + n].rearrange("e p k n -> (e p) k n"), KD, n)

            with sp.Fori(0, NE - 1) as p:
                expert_stream(p, p)
            sp.wait_ge(tab_ready, 1)
            last_pass = sp.value_load(lasti[0:1, 0:1], min_val=NE - 1, max_val=PASSES - 2)
            with sp.Fori(NE - 1, last_pass + 1) as p:
                e = sp.value_load(eidi[0:1, bass.ds(p, 1)], min_val=0, max_val=NE - 1)
                expert_stream(p, e)
            sp.wait_ge(sca_add, 4 * last_pass + 4)
            sp.dma_start(out[0].rearrange("(m p) d -> p m d", p=P), x[:, :, :]).then_inc(out_done, 16)
            sp.wait_ge(out_done, 16)

        @block.gpsimd
        def _(pool):
            pool.dma_start(posi[:, :], a['positions'][0].rearrange("(m p) -> p m", p=P),
                           allow_slow_non_contiguous=True).then_inc(pos_in, 16)

            def load_gain(k):
                if k:
                    pool.wait_ge(gain_free, 2 * k)
                src = a['attn_norm' if k % 2 == 0 else 'ffn_norm'][k // 2:k // 2 + 1, :]
                pool.dma_start(gain[:, :], src.to_broadcast([P, D])).then_inc(gain_in, 16)

            def row(dst, src, slow=False):
                pool.dma_start(dst, src, allow_slow_non_contiguous=slow).then_inc(param_in, 16)

            def load_params(l):
                def vec(name):
                    return a[name][l:l + 1, :]
                for i, w in enumerate('qk'):
                    row(bgain[:, i, :], vec(f'b_{w}n').to_broadcast([P, HD]))
                    row(cqkgain[:, i, :], vec(f'c_{w}n').to_broadcast([P, C_QK]))
                row(cngain[:, 0:CQ], vec('c_cq_norm').to_broadcast([P, CQ]))
                row(cngain[:, CQ:CQ + CKV], vec('c_ckv_norm').to_broadcast([P, CKV]))
                row(again[:, 0, :], vec('a_ln_g').to_broadcast([P, BW]))
                row(again[:, 1, :], vec('a_ln_b').to_broadcast([P, BW]))
                row(wsr[:, :, :], a['a_ws'][l].rearrange("g t s -> t g s"))
                row(abs_[:, :], a['a_bs'][l].rearrange("g t -> t g"), slow=True)
                row(uq[:, 0, :], a['c_w_uq'][l, 0:P, :])
                row(uq[0:CQ - P, 1, :], a['c_w_uq'][l, P:CQ, :])
                row(ukv[:, :], a['c_w_ukv'][l])
                row(cwr[0:D_CONV, :], a['d_conv_w'][l])
                for i, name in enumerate(('d_conv_b', 'd_ln_g', 'd_ln_b')):
                    row(dcol[:, i, :], a[name][l].rearrange("(c p) -> p c", p=P), slow=True)

            load_gain(0)
            nc.gpsimd.memset(ident[:, :], 0.0).then_inc(pool_seq, 1)
            nc.gpsimd.memset(tri384[:, :], 0.0).then_inc(pool_seq, 1)
            nc.gpsimd.memset(upper[:, :], 1.0).then_inc(pool_seq, 1)
            nc.gpsimd.memset(upstrict[:, :], 1.0).then_inc(pool_seq, 1)
            nc.gpsimd.memset(ones[:, :], 1.0)
            nc.gpsimd.memset(mean_w[:, :], 1.0 / BW)
            nc.gpsimd.memset(eps[:, :], EPS)
            for i in range(16):
                nc.gpsimd.memset(inv[:, i:i + 1], float(np.float32(THETA) ** np.float32(-2.0 * i / 32)))
            pool.wait_ge(pool_seq, 4)
            nc.gpsimd.affine_select(out=ident[:, :], in_=ident[:, :], compare_op=ALU.not_equal, fill=1.0, base=0,
                                    pattern=[[-1, P]], channel_multiplier=1)
            for c in (0, 256):
                nc.gpsimd.affine_select(out=tri384[:, c:c + P], in_=tri384[:, c:c + P], compare_op=ALU.is_ge,
                                        fill=NEG, base=0, pattern=[[-1, P]], channel_multiplier=1)
            nc.gpsimd.affine_select(out=upper[:, :], in_=upper[:, :], compare_op=ALU.is_ge, fill=0.0, base=0,
                                    pattern=[[1, P]], channel_multiplier=-1)
            nc.gpsimd.affine_select(out=upstrict[:, :], in_=upstrict[:, :], compare_op=ALU.is_gt, fill=0.0, base=0,
                                    pattern=[[1, P]], channel_multiplier=-1).then_inc(const_ready, 1)
            load_params(0)
            nc.gpsimd.iota(iotai[:, :], pattern=[[1, P]], base=0, channel_multiplier=0)
            nc.gpsimd.memset(before_e[:, :, :], 1.0).then_inc(pool_seq, 1)
            pool.wait_ge(pool_seq, 5)
            nc.gpsimd.affine_select(out=before_e[:, :, :], in_=before_e[:, :, :], compare_op=ALU.is_gt, fill=0.0,
                                    base=0, pattern=[[1, NE], [-1, NE]], channel_multiplier=0).then_inc(iota_ready, 1)
            pool.dma_start(wr[:, :, :], a['moe_router'][0].rearrange("(k p) e -> p k e", p=P)).then_inc(router_in, 16)
            pool.dma_start(rbias[:, :], a['moe_router_b'][0:1, :].to_broadcast([P, NE])).then_inc(router_in, 16)
            load_gain(1)
            pool.wait_ge(layer_done, 1)
            load_params(1)
            load_gain(2)
            load_gain(3)

        @block.tensor
        def _(pe):
            def transposed_h(k):
                for m in range(MT):
                    for g in range(2):
                        pe.wait_ge(h_ready, 4 * k + 2 * m + g + 1)
                        for j in range(4):
                            last = nc.tensor.transpose(bank[4 + m + 2 * g][:, P * j:P * (j + 1)],
                                                       hm[:, m, P * (4 * g + j):P * (4 * g + j + 1)], ident[:, :])
                        last.then_inc(hT_mm, 1)

            def prep(l):
                pe.wait_ge(param_in, 16 * N_PARAM * (l + 1))
                pe.wait_ge(hT_lo, 8 * l + 4)
                for g in range(4):
                    nc.tensor.transpose(bank[7][:, P * g:P * (g + 1)], wsr[:, g, :], ident[:, :])
                for c in range(2):
                    last = nc.tensor.transpose(bank[6][:, 32 * c:32 * c + D_CONV], cwr[0:D_CONV, P * c:P * (c + 1)],
                                               ident[0:D_CONV, 0:D_CONV])
                last.then_inc(wprep_mm, 1)

            def c_latent_T(l):
                pe.wait_ge(cn_ready, l + 1)
                pe.wait_ge(wprep_ev, l + 1)
                for m in range(MT):
                    o = P * m
                    nc.tensor.transpose(bank[4][:, o:o + P], cn[:, m, 0:P], ident[:, :])
                    nc.tensor.transpose(bank[4][:, 256 + o:256 + o + P], cn[:, m, CQ:CQ + CKV], ident[:, :])
                    last = nc.tensor.transpose(bank[5][0:CQ - P, o:o + P], cn[:, m, P:CQ], ident[:, :])
                last.then_inc(cnT_mm, 1)

            def c_up(l):
                pe.wait_ge(cnT_ev, l + 1)
                for m in range(MT):
                    t = slice(P * m, P * (m + 1))
                    nc.tensor.matmul(bank[4 + m][:, 0:384], cT[:, 0, t], uq[:, 0, :], start=True, stop=False)
                    nc.tensor.matmul(bank[4 + m][:, 0:384], cT[0:CQ - P, 2, t], uq[0:CQ - P, 1, :], start=False,
                                     stop=True)
                    last = nc.tensor.matmul(bank[6 + m][:, :], cT[:, 1, t], ukv[:, :], start=True, stop=True)
                last.then_inc(up_mm, 1)

            def c_qkT(l):
                pe.wait_ge(cqk_ready, l + 1)
                pe.wait_ge(up_ev, l + 1)
                for w, src in enumerate((ctq, kc)):
                    for hd in range(HEADS):
                        for m in range(MT):
                            b = bank[4 + 2 * w + hd // 2]
                            o = T * (hd % 2) + P * m
                            last = nc.tensor.transpose(b[0:C_QK, o:o + P], src[:, m, C_QK * hd:C_QK * (hd + 1)],
                                                       ident[:, :])
                    last.then_inc(qT_mm, 1)

            def b_qkT(l):
                pe.wait_ge(bqk_ready, l + 1)
                pe.wait_ge(o_lo[2], l + 1)
                for w in range(2):
                    for c in range(2):
                        for m in range(MT):
                            last = nc.tensor.transpose(bank[4 + w][:, T * c + P * m:T * c + P * (m + 1)],
                                                       prj[:, m, B_Q + BW * w + P * c:B_Q + BW * w + P * (c + 1)],
                                                       ident[:, :])
                    last.then_inc(qT_mm, 1)

            def scores(l, which):
                n = 2 * l + which
                pe.wait_ge(qT_evA, n + 1)
                pe.wait_ge(qT_evV, n + 1)
                if which:
                    pe.wait_ge(zpad_ready, l + 1)
                for hd in range(HEADS):
                    if which == 0:
                        q, k = qkT[0:C_QK, 0, hd, :], qkT[0:C_QK, 1, hd, :]
                    else:
                        o = HD * (hd % 2)
                        q = qkT[o:o + HD, 0, hd // 2, :]
                        k = qkT[o:o + HD, 0, 2 + hd // 2, :]
                    nc.tensor.matmul(bank[4 + hd][:, 0:P], q[:, 0:P], k[:, 0:P], start=True, stop=True)
                    nc.tensor.matmul(bank[4 + hd][:, P:384], q[:, P:T], k[:, 0:T], start=True,
                                     stop=True).then_inc(sc_mm, 1)

            def probs_T(l, which):
                n = 2 * l + which
                pe.wait_ge(pn_ready, n + 1)
                if which:
                    pe.wait_ge(az_ev, l + 1)
                for hd in range(HEADS):
                    for j in range(3):
                        last = nc.tensor.transpose(bank[4 + hd][:, P * j:P * (j + 1)],
                                                   probs[:, hd, P * j:P * (j + 1)], ident[:, :])
                    last.then_inc(pT_mm, 1)

            def values(l, which):
                n = 2 * l + which
                pe.wait_ge(pT_evA, 2 * n + 2)
                pe.wait_ge(pT_evV, 2 * n + 2)
                for hd in range(HEADS):
                    o = HD * (hd % 2)
                    c = T * (hd // 2)
                    if which == 0:
                        v = [ckv[:, m, 128 * hd + HD:128 * (hd + 1)] for m in range(MT)]
                    else:
                        v = [prj[:, m, B_V + HD * hd:B_V + HD * (hd + 1)] for m in range(MT)]
                    nc.tensor.matmul(bank[4][o:o + HD, c:c + T], v[0], pT[:, hd, 0:T], start=True, stop=False)
                    last = nc.tensor.matmul(bank[4][o:o + HD, c + P:c + T], v[1], pT[:, hd, T:384], start=False,
                                            stop=True)
                last.then_inc(o_mm[2 - which], 1)

            def d_zT(l):
                pe.wait_ge(glu_ready, l + 1)
                pe.wait_ge(pT_evV, 4 * l + 2)
                for c in range(2):
                    for m in range(MT):
                        last = nc.tensor.transpose(bank[6][:, T * c + P * m:T * c + P * (m + 1)],
                                                   dxc[:, m, P * c:P * (c + 1)], ident[:, :])
                last.then_inc(zT_mm, 1)

            def a_z(l):
                pe.wait_ge(vln_ready, l + 1)
                pe.wait_ge(sc_ev, 8 * l + 8)
                for m in range(MT):
                    for g in range(4):
                        o = BW * m + HD * g
                        last = nc.tensor.matmul(bank[4][:, o:o + HD], wsT[:, g, :],
                                                prj[:, m, A_V + HD * g:A_V + HD * (g + 1)], start=True, stop=True)
                last.then_inc(az_mm, 1)

            def a_oT(l):
                pe.wait_ge(pT_evV, 4 * l + 4)
                for c in range(2):
                    for m in range(MT):
                        last = nc.tensor.transpose(bank[6][:, T * c + P * m:T * c + P * (m + 1)],
                                                   prj[:, m, A_U + P * c:A_U + P * (c + 1)], ident[:, :])
                last.then_inc(o_mm[0], 1)

            def d_mean(l, src, ready, done, b):
                pe.wait_ge(ready, l + 1)
                for c in range(2):
                    last = nc.tensor.matmul(bank[b][:, 0:T], mean_w[:, :], src[:, c, :], start=(c == 0),
                                            stop=(c == 1))
                last.then_inc(done, 1)

            def tile_by_tile(pc, tokens):
                w = [w_half(pe, pc, hf, HALF, D) for hf in range(2)]
                for m in range(MT):
                    for c in range(2):
                        for hf in range(2):
                            sh, sl = tokens(m, hf)
                            o = slice(512 * c, 512 * (c + 1))
                            last = mm3(bank[2 * m + c][:, :], sh, sl, w[hf][0][:, 0, o], w[hf][1][:, 0, o], False,
                                       hf == 1)
                            if m == 1 and c == 1:
                                last.then_inc(w_used, 1)
                    if m == 0:
                        last.then_inc(m0_done, 1)

            def mixer(l):
                pcs = mixer_pieces(l)

                def proj_piece(ci, s):
                    c0, n = chunk_cols(ci)
                    slots = chunk_pieces(ci)
                    kk = KD // len(slots)
                    k0 = kk * slots.index(s)
                    if s == slots[0] and ci >= 2:
                        pe.wait_ge(prj_ev, n_chunk * l + ci - 1)
                    b = 2 * (ci % 2)
                    for hf in range(2):
                        wh, wl = w_half(pe, pcs[s], hf, kk // 2 * n, n)
                        for j in range(kk // 2):
                            k = k0 + kk // 2 * hf + j
                            for m in range(MT):
                                t = slice(P * m, P * (m + 1))
                                last = mm3(bank[b + m][:, 0:n], hTh[:, k, t], hTl[:, k, t], wh[:, j, :],
                                           wl[:, j, :], k == 0, k == KD - 1)
                        last.then_inc(w_used, 1)

                def small(s):
                    if s == 2:
                        prep(l)
                    if s == 4:
                        c_latent_T(l)
                    if s == 5:
                        c_up(l)
                    if s == 8:
                        c_qkT(l)
                    if s == 9:
                        scores(l, 0)
                    if s == 11:
                        probs_T(l, 0)
                    if s == 12:
                        values(l, 0)
                        d_zT(l)
                    if s == 13:
                        b_qkT(l)
                    if s == 14:
                        scores(l, 1)
                    if s == 15:
                        a_z(l)
                    if s == 16:
                        probs_T(l, 1)
                    if s == 17:
                        values(l, 1)
                        a_oT(l)
                    if s == 23:
                        d_mean(l, dacc, conv_ready, dmean_mm, 7)
                    if s == 24:
                        d_mean(l, zpad[:, :, 0:T], dsq_ready, dvar_mm, 5)

                for ci in range(n_chunk):
                    for s in chunk_pieces(ci):
                        if s < 2:
                            pe.wait_ge(hT_lo, 8 * l + 2 * s + 2)
                        proj_piece(ci, s)
                        small(s)

                for n in range(NB):
                    pe.wait_ge(o_lo[n], l + 1)
                    if n == 0:
                        pe.wait_ge(prj_ev, n_chunk * (l + 1))
                    if n == 1:
                        pe.wait_ge(dms_root, l + 1)
                    for c in range(2):
                        if n >= 2:
                            pe.wait_ge(br_ev, 4 * (NB * l + n - 2) + 2 * c + 2)
                        wh, wl = w_half(pe, pcs[25 + n], c, HALF, 512)
                        for m in range(MT):
                            t = slice(P * m, P * (m + 1))
                            for k in range(2):
                                last = mm3(bank[4 * (n % 2) + 2 * c + m][:, :], oTh[:, n, k, t], oTl[:, n, k, t],
                                           wh[:, k, :], wl[:, k, :], k == 0, k == 1)
                        last.then_inc(w_used, 1)

                def merged_T(g):
                    for m in range(MT):
                        pe.wait_ge(br_ev, 4 * (NB * l + 3) + 2 * g + m + 1)
                        for j in range(4):
                            last = nc.tensor.transpose(bank[4 + 2 * g + m][:, P * j:P * (j + 1)],
                                                       hm[:, m, P * (4 * g + j):P * (4 * g + j + 1)], ident[:, :])
                        last.then_inc(yT_mm, 1)

                merged_T(0)
                pe.wait_ge(yT_lo, 4 * l + 2)
                for j in range(3):
                    if j == 2:
                        pe.wait_ge(yT_lo, 4 * l + 4)
                    for hf in range(2):
                        wh, wl = w_half(pe, pcs[29 + j], hf, HALF, D)
                        k = 2 * j + hf
                        for m in range(MT):
                            t = slice(P * m, P * (m + 1))
                            for c in range(2):
                                last = mm3(bank[2 * m + c][:, :], hTh[:, k, t], hTl[:, k, t],
                                           wh[:, 0, 512 * c:512 * (c + 1)], wl[:, 0, 512 * c:512 * (c + 1)],
                                           k == 0, k == KD - 1)
                        last.then_inc(w_used, 1)
                    if j == 0:
                        merged_T(1)

                tile_by_tile(pcs[32], lambda m, hf: (hTh[:, 6 + hf, P * m:P * (m + 1)],
                                                     hTl[:, 6 + hf, P * m:P * (m + 1)]))

            def gate_up(pc, col, n, out_bank, st_h, st_l, tiles, first=False):
                for hf in range(2):
                    if first:
                        pe.wait_ge(hT_lo, 4 + 2 * hf + 2)
                    wh, wl = w_half(pe, pc, hf, 4 * n, n)
                    for j in range(4):
                        k = 4 * hf + j
                        for m in range(tiles):
                            t = slice(P * m, P * (m + 1))
                            last = mm3(out_bank(m)[:, col:col + n], st_h[:, k, t], st_l[:, k, t], wh[:, j, :],
                                       wl[:, j, :], k == 0, k == KD - 1)
                    last.then_inc(w_used, 1)

            def ffn():
                gu = lambda m: bank[4 + m]

                def step_gu(i, pg, pu, first=False):
                    if not first:
                        pe.wait_ge(act_ready, i)
                    gate_up(pg, 0, FSTEP, gu, hTh, hTl, MT, first)
                    gate_up(pu, FSTEP, FSTEP, gu, hTh, hTl, MT)

                def step_T(i, par):
                    pe.wait_ge(act_ready, i + 1)
                    for k in range(2):
                        for m in range(MT):
                            last = nc.tensor.transpose(bank[6 + par][:, T * k + P * m:T * k + P * (m + 1)],
                                                       act[:, m, P * k:P * (k + 1)], ident[:, :])
                    last.then_inc(aT_mm, 1)

                def step_down(i, pd, par, start, stop):
                    pe.wait_ge(aT_lo, i + 1)
                    for hf in range(2):
                        wh, wl = w_half(pe, pd, hf, HALF, D)
                        for m in range(MT):
                            t = slice(P * m, P * (m + 1))
                            for c in range(2):
                                last = mm3(bank[2 * m + c][:, :], aTh[par][:, hf, t], aTl[par][:, hf, t],
                                           wh[:, 0, 512 * c:512 * (c + 1)], wl[:, 0, 512 * c:512 * (c + 1)],
                                           start and hf == 0, stop and hf == 1)
                        last.then_inc(w_used, 1)

                step_gu(0, Piece(FFN_BASE), Piece(FFN_BASE + 1), first=True)
                step_T(0, 0)

                def body(i, par, first, it, per, start=False):
                    step_gu(i, Piece(first, it, per), Piece(first + 1, it, per))
                    step_down(i - 1, Piece(first + 2, it, per), 1 - par, start, False)
                    step_T(i, par)

                body(1, 1, FFN_BASE + 2, 0, 0, start=True)
                body(2, 0, FFN_BASE + 5, 0, 0)
                with pe.Fori(0, 3) as it:
                    for r in range(2):
                        body(2 * it + 3 + r, (3 + r) % 2, FFN_BASE + 8 + 3 * r, it, 6)
                for i in (9, 10):
                    body(i, i % 2, FFN_BASE + 2 + 3 * (i - 1), 0, 0)
                pe.wait_ge(aT_lo, 11)
                tile_by_tile(Piece(FFN_BASE + 32), lambda m, hf: (aTh[0][:, hf, P * m:P * (m + 1)],
                                                                  aTl[0][:, hf, P * m:P * (m + 1)]))

            def router():
                pe.wait_ge(hT_lo, 16)
                pe.wait_ge(wr_lo, 1)
                o = bank[7][0:NE, 0:T]
                for k in range(KD):
                    nc.tensor.matmul(o, wrh[:, k, :], hTh[:, k, :], start=(k == 0), stop=False)
                    nc.tensor.matmul(o, wrh[:, k, :], hTl[:, k, :], start=False, stop=False)
                    last = nc.tensor.matmul(o, wrl[:, k, :], hTh[:, k, :], start=False, stop=(k == KD - 1))
                last.then_inc(lg_mm, 1)
                pe.wait_ge(lgT_ev, 1)
                for m in range(MT):
                    last = nc.tensor.transpose(bank[6][:, 32 + 8 * m:40 + 8 * m], lgT[0:NE, P * m:P * (m + 1)],
                                               ident[0:NE, 0:NE])
                last.then_inc(lgT_mm, 1)
                pe.wait_ge(member_ready, 1)
                mem = [tab[:, 2 + m, 0:NE] for m in range(MT)]
                nc.tensor.matmul(bank[6][:, 0:8], upstrict[:, :], mem[0], start=True, stop=True)
                nc.tensor.matmul(bank[6][:, 8:16], upstrict[:, :], mem[1], start=True, stop=False)
                nc.tensor.matmul(bank[6][:, 8:16], ones[:, :], mem[0], start=False, stop=True)
                nc.tensor.matmul(bank[6][:, 16:24], ones[:, :], mem[0], start=True, stop=False)
                nc.tensor.matmul(bank[6][:, 16:24], ones[:, :], mem[1], start=False, stop=True).then_inc(rank_mm, 1)

            def gather(q, halves=(0, 1)):
                pe.wait_ge(pick_ready, q + 1)
                for k in range(4 * halves[0], 4 * halves[-1] + 4):
                    o = bank[5 + k // 4][:, P * (k % 4):P * (k % 4 + 1)]
                    for m in range(MT):
                        c = slice(P * k, P * (k + 1))
                        nc.tensor.matmul(o, htokh[:, m, c], pick[:, m, :], start=(m == 0), stop=False)
                        last = nc.tensor.matmul(o, htokl[:, m, c], pick[:, m, :], start=False, stop=(m == MT - 1))
                    if k % 4 == 3:
                        last.then_inc(gat_mm, 1)

            def slot_rows(p):
                for m in range(MT):
                    nc.tensor.transpose(bank[7][:, P * m:P * (m + 1)], pickf[:, m, :], ident[:, :])
                for m in range(MT):
                    last = nc.tensor.matmul(bank[7][:, T:T + 1], pickf[:, m, :], wcol[:, m:m + 1], start=(m == 0),
                                            stop=(m == MT - 1))
                last.then_inc(pick_mm, 1)

            def scatter(q):
                pe.wait_ge(y_lo, 2 * q + 2)
                for m in range(MT):
                    for c in range(2):
                        o = bank[(0, 5)[m] + c][:, :]
                        r = slice(512 * c, 512 * (c + 1))
                        nc.tensor.matmul(o, pickT[:, P * m:P * (m + 1)], yh[:, r], start=True, stop=False)
                        nc.tensor.matmul(o, pickT[:, P * m:P * (m + 1)], yl[:, r], start=False,
                                         stop=True).then_inc(sca_mm, 1)

            def expert_pass(p, before=None):
                first = before is None
                pe.wait_ge(gat_lo, 2 * p + 2)

                def down(s, pc):
                    pe.wait_ge(e_aT_lo, 6 * p + s + 1)
                    if s == 0 and not first:
                        pe.wait_ge(sca_add, 4 * before + 2)
                    nk = ESTEPS[s] // P
                    for hf in range(2):
                        wh, wl = w_half(pe, pc, hf, nk * D // 2, 512)
                        for c in range(nk):
                            k, cc = (hf, c) if nk == 2 else (0, hf)
                            last = mm3(bank[cc][:, :], aTh[s % 2][:, k, 0:P], aTl[s % 2][:, k, 0:P], wh[:, c, :],
                                       wl[:, c, :], s == 0 and k == 0, s == 5)
                        last.then_inc(w_used, 1)

                def paired_gate_up(pc, k0, n, out_bank):
                    for hf in range(2):
                        wh, wl = w_half(pe, pc, hf, 4 * n, 2 * n)
                        for j in range(2):
                            k = k0 + 2 * hf + j
                            last = mm3(out_bank[:, 0:2 * n], xgh[:, k, :], xgl[:, k, :], wh[:, j, :], wl[:, j, :],
                                       k == 0, k == KD - 1)
                        last.then_inc(w_used, 1)

                def turn(s):
                    pe.wait_ge(e_act, 6 * p + s + 1)
                    for k in range(ESTEPS[s] // P):
                        last = nc.tensor.transpose(bank[4][:, P * k:P * (k + 1)], act[:, 0, P * k:P * (k + 1)],
                                                   ident[:, :])
                    last.then_inc(e_aT_mm, 1)

                for j, (kind, s) in enumerate(ORDER):
                    pc = Piece(MOE_BASE + j, p, PASS_PIECES, experts=True)
                    n = ESTEPS[s]
                    gu = lambda m: bank[2 + s % 2]
                    if kind == "d":
                        down(s, pc)
                        if s < 5:
                            turn(s + 1)
                        if s == 4:
                            gather(p + 1, (1,))
                        continue
                    if s == 5:
                        paired_gate_up(pc, 0 if kind == "g" else KD // 2, n, gu(0))
                    else:
                        gate_up(pc, 0 if kind == "g" else n, n, gu, xgh, xgl, 1)
                    if kind == "u" and s == 0:
                        if not first:
                            scatter(before)
                        slot_rows(p)
                        turn(0)
                    if kind == "u" and s == 5:
                        gather(p + 1, (0,))

            pe.wait_ge(const_ready, 1)
            transposed_h(0)
            mixer(0)
            transposed_h(1)
            ffn()
            transposed_h(2)
            mixer(1)
            transposed_h(3)
            router()
            gather(0)
            expert_pass(0)
            pe.wait_ge(tab_ready, 1)
            last_pass = pe.value_load(lasti[0:1, 0:1], min_val=NE - 1, max_val=PASSES - 2)
            with pe.Fori(0, last_pass) as r:
                expert_pass(r + 1, before=r)
            scatter(last_pass)

        @block.scalar
        def _(act_e):
            own = [0]

            def link(ins):
                own[0] += 1
                ins.then_inc(act_seq, 1)
                act_e.wait_ge(act_seq, own[0])

            def square_sum(k, m):
                idle = gates[:, 1, (2 + m) * D:(3 + m) * D] if k < 3 else squares[:, m, :]
                return nc.scalar.activation(idle, x[:, m, :], ACT.Square, accum_out=ssum[:, m:m + 1])

            def norm_upper(k, m):
                for g in range(2):
                    act_e.wait_ge(hT_mm, 4 * k + 2 * m + g + 1)
                    nc.scalar.copy(hTh[:, 4 * g:4 * g + 4, P * m:P * (m + 1)],
                                   bank[4 + m + 2 * g][:, :].rearrange("p (k t) -> p k t", t=P)).then_inc(hT_hi, 1)

            def token_norm(k, piece=None):
                if k == 0:
                    norm_upper(k, 0)
                    norm_upper(k, 1)
                    split_hi(act_e, Piece(0))
                    split_hi(act_e, Piece(1))
                    link(square_sum(k, 0))
                else:
                    act_e.wait_ge(x_new, 4 * (k - 1) + 2)
                    square_sum(k, 0)
                    norm_upper(k, 0)
                    norm_upper(k, 1)
                if 0 < k < 3:
                    split_hi(act_e, piece)
                link(square_sum(k, 1))
                nc.scalar.activation(rstd[:, 0, :], ssum[:, :], ACT.Sqrt, bias=eps[:, 0:1],
                                     scale=1.0 / D).then_inc(rms_root, 1)
                if k == 3:
                    split_hi(act_e, piece)

            def attention_exp(l, which):
                act_e.wait_ge(mx_ready, 2 * l + which + 1)
                for m in range(MT):
                    for hd in range(HEADS):
                        seg = probs[:, hd, 0:P] if m == 0 else probs[:, hd, P:384]
                        last = nc.scalar.activation(seg, seg, ACT.Exp, bias=stat[:, 4 * m + hd:4 * m + hd + 1],
                                                    accum_out=stat[:, 8 + 4 * m + hd:9 + 4 * m + hd])
                last.then_inc(ex_done, 1)

            def probs_T_ev(l, which):
                n = 2 * l + which
                for hd in range(2):
                    act_e.wait_ge(pT_mm, 4 * n + hd + 1)
                    nc.scalar.copy(pT[:, hd, :], bank[4 + hd][:, 0:384]).then_inc(pT_evA, 1)

            def o_upper(l, n, b):
                act_e.wait_ge(o_mm[n], l + 1)
                nc.scalar.copy(oTh[:, n, :, :], bank[b][:, :].rearrange("p (c t) -> p c t", t=T)).then_inc(o_hi[n], 1)

            def gate_sigmoid(l, n):
                act_e.wait_ge(prj_ev, n_chunk * l + 5 + 2 * (n + 1))
                for m in range(MT):
                    g = gates[:, m, D * n:D * (n + 1)]
                    nc.scalar.activation(g, g, ACT.Sigmoid).then_inc(gate_sig, 1)

            def mixer(l):
                pcs = mixer_pieces(l)
                last_of = {chunk_pieces(ci)[-1]: ci for ci in range(n_chunk)}

                def chunk_ev(ci):
                    c0, n = chunk_cols(ci)
                    act_e.wait_ge(w_used, 2 * pcs[chunk_pieces(ci)[-1]].number + 2)
                    if ci == 0:
                        act_e.wait_ge(rstd_ready, 2 * l + 1)
                    for m in range(MT):
                        dst = prj[:, m, c0 - GATES:c0 - GATES + n] if ci < 5 else gates[:, m, c0:c0 + n]
                        last = nc.scalar.mul(dst, bank[2 * (ci % 2) + m][:, 0:n], rstd[:, 1, m:m + 1])
                    last.then_inc(prj_ev, 1)

                def merged_upper(g):
                    for m in range(MT):
                        act_e.wait_ge(yT_mm, 4 * l + 2 * g + m + 1)
                        nc.scalar.copy(hTh[:, 4 * g:4 * g + 4, P * m:P * (m + 1)],
                                       bank[4 + 2 * g + m][:, :].rearrange("p (k t) -> p k t", t=P)).then_inc(yT_hi, 1)

                for s in range(MIX_PIECES):
                    if s == 28:
                        merged_upper(0)
                    if s + 2 < MIX_PIECES:
                        split_hi(act_e, pcs[s + 2], piece_half(s + 2))
                    elif s + 2 == MIX_PIECES:
                        split_hi(act_e, after_mixer(l, 0))
                    if s in last_of:
                        chunk_ev(last_of[s])
                    if s == 3:
                        act_e.wait_ge(cms, l + 1)
                        nc.scalar.activation(stat[:, 16:18], stat[:, 16:18], ACT.Sqrt, bias=eps[:, 0:1], scale=1.0 / CQ)
                        nc.scalar.activation(stat[:, 18:20], stat[:, 18:20], ACT.Sqrt, bias=eps[:, 0:1],
                                             scale=1.0 / CKV).then_inc(cms_root, 1)
                    if s == 4:
                        act_e.wait_ge(cnT_mm, l + 1)
                        nc.scalar.copy(cT[:, 0:2, :], bank[4][:, :].rearrange("p (c t) -> p c t", t=T))
                        nc.scalar.copy(cT[0:CQ - P, 2, :], bank[5][0:CQ - P, 0:T]).then_inc(cnT_ev, 1)
                    if s == 5:
                        act_e.wait_ge(up_mm, l + 1)
                        for m in range(MT):
                            nc.scalar.copy(ctq[:, m, :], bank[4 + m][:, 0:384])
                            last = nc.scalar.copy(ckv[:, m, :], bank[6 + m][:, :])
                        last.then_inc(up_ev, 1)
                    if s == 6:
                        act_e.wait_ge(qms, l + 1)
                        nc.scalar.activation(stat[:, 20:36], stat[:, 20:36], ACT.Sqrt, bias=eps[:, 0:1],
                                             scale=1.0 / C_QK).then_inc(qms_root, 1)
                    if s == 8:
                        act_e.wait_ge(ams, l + 1)
                        nc.scalar.activation(stat[:, 40:44:2], stat[:, 41:45:2], ACT.Sqrt,
                                             bias=eps[:, 0:1]).then_inc(ams_root, 1)
                        act_e.wait_ge(qT_mm, 4 * l + 1)
                        for c in range(2):
                            last = nc.scalar.copy(qkT[0:C_QK, 0, 2 * c:2 * c + 2, :],
                                                  bank[4 + c][0:C_QK, :].rearrange("p (h t) -> p h t", t=T))
                        last.then_inc(qT_evA, 1)
                    if s == 9:
                        attention_exp(l, 0)
                    if s == 10:
                        g = prj[:, :, D_G:D_G + BW]
                        nc.scalar.activation(g, g, ACT.Sigmoid).then_inc(glu_sig, 1)
                    if s == 11:
                        probs_T_ev(l, 0)
                        act_e.wait_ge(bms, l + 1)
                        nc.scalar.activation(stat[:, 20:36], stat[:, 20:36], ACT.Sqrt, bias=eps[:, 0:1],
                                             scale=1.0 / HD).then_inc(bms_root, 1)
                    if s == 12:
                        o_upper(l, 2, 4)
                        act_e.wait_ge(zT_mm, l + 1)
                        nc.scalar.copy(zpad[:, :, D_CONV - 1:D_CONV - 1 + T],
                                       bank[6][:, :].rearrange("p (c t) -> p c t", t=T)).then_inc(zpad_ready, 1)
                    if s == 13:
                        act_e.wait_ge(qT_mm, 4 * l + 3)
                        nc.scalar.copy(qkT[:, 0, 0:2, :],
                                       bank[4][:, :].rearrange("p (h t) -> p h t", t=T)).then_inc(qT_evA, 1)
                    if s == 14:
                        attention_exp(l, 1)
                    if s == 16:
                        probs_T_ev(l, 1)
                    if s == 17:
                        o_upper(l, 1, 4)
                        o_upper(l, 0, 6)
                    if s == 22:
                        gate_sigmoid(l, 0)
                        gate_sigmoid(l, 1)
                    if s == 24:
                        act_e.wait_ge(dvar_mm, l + 1)
                        nc.scalar.activation(dsd, bank[5][:, 0:T], ACT.Sqrt, bias=eps[:, 0:1]).then_inc(dms_root, 1)
                        act_e.wait_ge(dlin_ready, l + 1)
                        nc.scalar.activation(zpad[:, :, 0:T], dxc[:, :, :], ACT.Sigmoid).then_inc(dsig_ready, 1)
                        gate_sigmoid(l, 2)
                    if s == 25:
                        act_e.wait_ge(do_ready, l + 1)
                        nc.scalar.copy(oTh[:, 3, :, :], dacc[:, :, :]).then_inc(o_hi[3], 1)
                        gate_sigmoid(l, 3)
                    if s == 29:
                        merged_upper(1)

            def ffn():
                def sigmoid(i, pu):
                    act_e.wait_ge(w_used, 2 * pu.number + 2)
                    for m in range(MT):
                        nc.scalar.activation(sig[:, m, :], bank[4 + m][:, 0:FSTEP], ACT.Sigmoid,
                                             scale=rstd[:, 1, m:m + 1]).then_inc(sig_ready, 1)

                def turned(i, par):
                    act_e.wait_ge(aT_mm, i + 1)
                    nc.scalar.copy(aTh[par][:, :, :],
                                   bank[6 + par][:, :].rearrange("p (k t) -> p k t", t=T)).then_inc(aT_hi, 1)

                def body(i, par, first, it, per, ahead=True):
                    pu = Piece(first + 1, it, per)
                    split_hi(act_e, pu)
                    split_hi(act_e, Piece(first + 2, it, per))
                    sigmoid(i, pu)
                    if ahead:
                        split_hi(act_e, Piece(first + 3, it, per))
                    turned(i, par)

                act_e.wait_ge(rstd_ready, 2)
                sigmoid(0, Piece(FFN_BASE + 1))
                split_hi(act_e, Piece(FFN_BASE + 2))
                turned(0, 0)
                with act_e.Fori(0, 4) as it:
                    for r in range(2):
                        body(2 * it + 1 + r, (1 + r) % 2, FFN_BASE + 2 + 3 * r, it, 6)
                body(9, 1, FFN_BASE + 26, 0, 0)
                body(10, 0, FFN_BASE + 29, 0, 0, ahead=False)
                for j in range(2):
                    split_hi(act_e, Piece(FFN_BASE + 32 + j))

            def expert_pass(p, before=None):
                first = before is None
                def pc(j):
                    return Piece(MOE_BASE + j, p, PASS_PIECES, experts=True)

                def half(j):
                    return ESTEPS[ORDER[j][1]] * 4

                def turned(s):
                    act_e.wait_ge(e_aT_mm, 6 * p + s + 1)
                    nk = ESTEPS[s] // P
                    nc.scalar.copy(aTh[s % 2][:, 0:nk, 0:P],
                                   bank[4][:, 0:ESTEPS[s]].rearrange("p (k t) -> p k t", t=P)).then_inc(e_aT_hi, 1)

                if not first:
                    split_hi(act_e, pc(0))
                    split_hi(act_e, pc(1))
                    rows_upper(before)
                for j, (kind, s) in enumerate(ORDER):
                    if kind == "u":
                        act_e.wait_ge(w_used, 2 * pc(j).number + 2)
                        nc.scalar.activation(sig[:, 0, 0:ESTEPS[s]], bank[2 + s % 2][:, 0:ESTEPS[s]],
                                             ACT.Sigmoid).then_inc(e_sig, 1)
                    if j + 2 < PASS_PIECES:
                        split_hi(act_e, pc(j + 2), half(j + 2))
                    if kind == "u" and s == 0:
                        act_e.wait_ge(pick_mm, p + 1)
                        nc.scalar.copy(pickT[:, :], bank[7][:, 0:T]).then_inc(pickT_ev, 1)
                        turned(0)
                    if kind == "u" and s == 5:
                        gathered_upper(p + 1, (0,))
                    if kind == "d" and s < 5:
                        turned(s + 1)
                    if j == PASS_PIECES - 2:
                        gathered_upper(p + 1, (1,))

            def gathered_upper(q, halves=(0, 1)):
                for g in halves:
                    act_e.wait_ge(gat_mm, 2 * q + g + 1)
                    nc.scalar.copy(xgh[:, 4 * g:4 * g + 4, :],
                                   bank[5 + g][:, :].rearrange("p (k t) -> p k t", t=P)).then_inc(gat_hi, 1)

            def rows_upper(q):
                act_e.wait_ge(w_used, 2 * (MOE_BASE + PASS_PIECES) + 2 * PASS_PIECES * q)
                act_e.wait_ge(wslot_ready, q + 1)
                for c in range(2):
                    nc.scalar.mul(yh[:, 512 * c:512 * (c + 1)], bank[c][:, :], wslot[:, 0:1]).then_inc(y_hi, 1)

            act_e.wait_ge(const_ready, 1)
            token_norm(0)
            act_e.wait_ge(ang_ready, 2)
            nc.scalar.activation(sinT[:, :, :], sinT[:, :, :], ACT.Sin)
            nc.scalar.activation(cosT[:, :, :], cosT[:, :, :], ACT.Sin).then_inc(trig_ready, 1)
            mixer(0)
            token_norm(1, after_mixer(0, 1))
            act_e.wait_ge(router_in, 32)
            nc.scalar.copy(wrh[:, :, :], wr[:, :, :]).then_inc(wr_hi, 1)
            ffn()
            token_norm(2, Piece(FFN_BASE + 34))
            mixer(1)
            token_norm(3, after_mixer(1, 1))
            act_e.wait_ge(lg_mm, 1)
            nc.scalar.copy(lgT[0:NE, :], bank[7][0:NE, 0:T]).then_inc(lgT_ev, 1)
            act_e.wait_ge(rstd_ready, 4)
            for m in range(MT):
                nc.scalar.mul(htokh[:, m, :], hm[:, m, :], rstd[:, 1, m:m + 1]).then_inc(tok_hi, 1)
            act_e.wait_ge(diff_ready, 1)
            nc.scalar.activation(wtop[:, :, :], diff[:, :, :], ACT.Sigmoid).then_inc(wtop_ready, 1)
            gathered_upper(0)
            expert_pass(0)
            act_e.wait_ge(tab_ready, 1)
            last_pass = act_e.value_load(lasti[0:1, 0:1], min_val=NE - 1, max_val=PASSES - 2)
            with act_e.Fori(0, last_pass) as r:
                expert_pass(r + 1, before=r)
            rows_upper(last_pass)

        @block.vector
        def _(dve):
            own = [0]

            def link(ins):
                own[0] += 1
                ins.then_inc(dve_seq, 1)
                dve.wait_ge(dve_seq, own[0])

            V = nc.vector

            def lower_hT(done, hi, count, halves=(0, 1)):
                for g in halves:
                    for m in range(MT):
                        dve.wait_ge(hi, count(m, g))
                        o = slice(P * m, P * (m + 1))
                        V.tensor_tensor(hTl[:, 4 * g:4 * g + 4, o],
                                        bank[4 + m + 2 * g][:, :].rearrange("p (k t) -> p k t", t=P),
                                        hTh[:, 4 * g:4 * g + 4, o].bitcast(F32), ALU.subtract).then_inc(done, 1)

            def token_norm(k, last_piece=None, stage=0, piece=None):
                dve.wait_ge(gain_in, 16 * (k + 1))
                for m in range(MT):
                    if k == 0:
                        dve.wait_ge(x_in[m], 16)
                    elif m == 0:
                        dve.wait_ge(m0_done, stage)
                    else:
                        dve.wait_ge(w_used, 2 * last_piece.number + 2)
                    for c in range(2):
                        cols = slice(512 * c, 512 * (c + 1))
                        o = x[:, m, cols]
                        if k:
                            V.tensor_tensor(o, o, bank[2 * m + c][:, :], ALU.add).then_inc(x_new, 1)
                            dve.wait_ge(x_new, 4 * (k - 1) + 2 * m + c + 1)
                        V.tensor_tensor(hm[:, m, cols], o, gain[:, cols], ALU.mult).then_inc(h_ready, 1)
                V.engine_nop().then_inc(gain_free, 2)
                lower_hT(hT_lo, hT_hi, lambda m, g: 4 * k + 2 * m + g + 1)
                if k == 0:
                    split_lo(dve, Piece(0))
                    split_lo(dve, Piece(1))
                elif k < 3:
                    split_lo(dve, piece)
                dve.wait_ge(rms_root, k + 1)
                V.reciprocal(rstd[:, 1, :], rstd[:, 0, :]).then_inc(rstd_ready, 1)
                if k == 3:
                    split_lo(dve, piece)

            def angles():
                two_pi = 2 * np.pi
                c1 = 6.28125
                c2 = float(np.float32(np.round((two_pi - c1) * 2 ** 21) / 2 ** 21))
                c3 = float(np.float32(two_pi - c1 - c2))
                magic = 1.5 * 2 ** 23
                ang, turns, r, neg = (dacc[:, 0, 32 * i:32 * (i + 1)] for i in range(4))
                link(V.tensor_copy(posf[:, :], posi[:, :]))
                for m in range(MT):
                    last = V.tensor_scalar(ang[:, 16 * m:16 * (m + 1)], inv[:, :], posf[:, m:m + 1], None, ALU.mult)
                link(last)
                link(V.tensor_scalar(turns, ang, 1.0 / two_pi, magic, ALU.mult, ALU.add))
                link(V.tensor_scalar(turns, turns, magic, None, ALU.subtract))
                link(V.scalar_tensor_tensor(out=r, in0=turns, scalar=-c1, in1=ang, op0=ALU.mult, op1=ALU.add))
                link(V.scalar_tensor_tensor(out=r, in0=turns, scalar=-c2, in1=r, op0=ALU.mult, op1=ALU.add))
                link(V.scalar_tensor_tensor(out=r, in0=turns, scalar=-c3, in1=r, op0=ALU.mult, op1=ALU.add))
                flat = sinT[:, :, :].rearrange("p m i -> p (m i)")
                V.tensor_scalar(flat, r, 3.1415925, -3.1415925, ALU.min, ALU.max).then_inc(ang_ready, 1)
                dve.wait_ge(ang_ready, 1)
                link(V.scalar_tensor_tensor(out=neg, in0=flat, scalar=-1.0, in1=flat, op0=ALU.mult, op1=ALU.max))
                V.tensor_scalar(cosT[:, :, :].rearrange("p m i -> p (m i)"), neg, -1.0, float(np.pi / 2), ALU.mult,
                                ALU.add).then_inc(ang_ready, 1)

            def rope(x1, x2, step, tmp, heads, r2):
                t = [tmp[:, i * MT * heads * r2:(i + 1) * MT * heads * r2].rearrange(
                    "p (m h r) -> p m h r", m=MT, h=heads) for i in range(4)]
                c = cosT[:, :, ::step].unsqueeze(2).to_broadcast([P, MT, heads, r2])
                s = sinT[:, :, ::step].unsqueeze(2).to_broadcast([P, MT, heads, r2])
                V.tensor_tensor(t[0], x1, c, ALU.mult)
                V.tensor_tensor(t[1], x2, s, ALU.mult)
                V.tensor_tensor(t[2], x2, c, ALU.mult)
                link(V.tensor_tensor(t[3], x1, s, ALU.mult))
                V.tensor_tensor(x1, t[0], t[1], ALU.subtract)
                link(V.tensor_tensor(x2, t[2], t[3], ALU.add))

            def prep(l):
                dve.wait_ge(wprep_mm, l + 1)
                V.tensor_tensor(wsT[:, :, :], bank[7][:, :].rearrange("p (g t) -> p g t", t=P),
                                upper[:, :].unsqueeze(1).to_broadcast([P, 4, P]), ALU.mult)
                V.memset(zpad[:, :, 0:D_CONV - 1], 0.0)
                V.tensor_copy(cw[:, :, :], bank[6][:, 0:64].rearrange("p (c j) -> p c j", c=2)[:, :, 0:D_CONV]
                              ).then_inc(wprep_ev, 1)

            def c_norm_latents(l):
                dve.wait_ge(param_in, 16 * N_PARAM * (l + 1))
                dve.wait_ge(prj_ev, n_chunk * l + 2)
                lat = prj[:, :, C_Q:C_Q + 320]
                sq = scr0[:, 0:640].rearrange("p (m c) -> p m c", m=MT)
                link(V.tensor_tensor(sq, lat, lat, ALU.mult))
                V.tensor_reduce(stat[:, 16:18], sq[:, :, 0:CQ], AX_X, ALU.add)
                V.tensor_reduce(stat[:, 18:20], sq[:, :, CQ:320], AX_X, ALU.add).then_inc(cms, 1)
                dve.wait_ge(cms_root, l + 1)
                link(V.reciprocal(stat[:, 16:20], stat[:, 16:20]))
                for m in range(MT):
                    V.scalar_tensor_tensor(out=cn[:, m, 0:CQ], in0=lat[:, m, 0:CQ], scalar=stat[:, 16 + m:17 + m],
                                           in1=cngain[:, 0:CQ], op0=ALU.mult, op1=ALU.mult)
                    last = V.scalar_tensor_tensor(out=cn[:, m, CQ:320], in0=lat[:, m, CQ:320],
                                                  scalar=stat[:, 18 + m:19 + m], in1=cngain[:, CQ:320],
                                                  op0=ALU.mult, op1=ALU.mult)
                last.then_inc(cn_ready, 1)

            def c_sum_qk(l):
                dve.wait_ge(up_ev, l + 1)
                q4 = ctq[:, :, :].rearrange("p m (h c) -> p m h c", h=HEADS)
                k4 = kc.rearrange("p m (h c) -> p m h c", h=HEADS)
                nope = ckv[:, :, :].rearrange("p m (h c) -> p m h c", h=HEADS)[:, :, :, 0:HD]
                kr = prj[:, :, C_R:C_R + CR].unsqueeze(2).to_broadcast([P, MT, HEADS, CR])
                sq = scr0[:, 0:MT * 384].rearrange("p (m h c) -> p m h c", m=MT, h=HEADS)
                V.tensor_copy(k4[:, :, :, 0:HD], nope)
                link(V.tensor_copy(k4[:, :, :, HD:C_QK], kr))
                for w, src in enumerate((q4, k4)):
                    link(V.tensor_tensor(sq, src, src, ALU.mult))
                    dst = stat[:, 20 + 8 * w:28 + 8 * w].rearrange("p (m h) -> p m h", m=MT)
                    last = V.tensor_reduce(dst, sq, AX_X, ALU.add)
                    if w == 0:
                        link(last)
                last.then_inc(qms, 1)

            def c_rotate_qk(l):
                q4 = ctq[:, :, :].rearrange("p m (h c) -> p m h c", h=HEADS)
                k4 = kc.rearrange("p m (h c) -> p m h c", h=HEADS)
                dve.wait_ge(qms_root, l + 1)
                link(V.reciprocal(stat[:, 20:36], stat[:, 20:36]))
                for w, src in enumerate((q4, k4)):
                    rs = stat[:, 20 + 8 * w:28 + 8 * w].rearrange("p (m h) -> p m h", m=MT)
                    V.tensor_tensor(src, src, rs.unsqueeze(3).to_broadcast([P, MT, HEADS, C_QK]), ALU.mult)
                link(V.engine_nop())
                if l == 0:
                    dve.wait_ge(trig_ready, 1)
                for w, src in enumerate((ctq[:, :, :], kc)):
                    src = src.rearrange("p m (h c) -> p (m h) c", h=HEADS)
                    last = V.tensor_tensor(src, src, cqkgain[:, w, :].unsqueeze(1).to_broadcast([P, MT * HEADS, C_QK]),
                                           ALU.mult)
                link(last)
                for src in (q4, k4):
                    rope(src[:, :, :, HD:HD + 16], src[:, :, :, HD + 16:C_QK], 1, scr0, HEADS, 16)
                V.engine_nop().then_inc(cqk_ready, 1)

            def b_sum_qk(l):
                qk = prj[:, :, B_Q:B_Q + 512]
                q8 = qk.rearrange("p m (h c) -> p m h c", h=8)
                sq = scr0.rearrange("p (m h c) -> p m h c", m=MT, h=8)
                link(V.tensor_tensor(sq, q8, q8, ALU.mult))
                V.tensor_reduce(stat[:, 20:36].rearrange("p (m h) -> p m h", m=MT), sq, AX_X,
                                ALU.add).then_inc(bms, 1)

            def b_rotate_qk(l):
                qk = prj[:, :, B_Q:B_Q + 512]
                q8 = qk.rearrange("p m (h c) -> p m h c", h=8)
                dve.wait_ge(bms_root, l + 1)
                link(V.reciprocal(stat[:, 20:36], stat[:, 20:36]))
                rs = stat[:, 20:36].rearrange("p (m h) -> p m h", m=MT)
                link(V.tensor_tensor(q8, q8, rs.unsqueeze(3).to_broadcast([P, MT, 8, HD]), ALU.mult))
                for m in range(MT):
                    src = qk[:, m, :].rearrange("p (w h c) -> p w h c", w=2, h=HEADS)
                    last = V.tensor_tensor(src, src, bgain[:, :, :].unsqueeze(2).to_broadcast([P, 2, HEADS, HD]),
                                           ALU.mult)
                link(last)
                rope(q8[:, :, :, 0:8], q8[:, :, :, 8:16], 2, scr1, 8, 8)
                V.engine_nop().then_inc(bqk_ready, 1)

            def softmax_start(l, which):
                scale = (C_QK if which == 0 else HD) ** -0.5
                n = 2 * l + which
                for hd in range(HEADS):
                    dve.wait_ge(sc_mm, 4 * n + hd + 1)
                    V.scalar_tensor_tensor(out=probs[:, hd, :], in0=bank[4 + hd][:, 0:384], scalar=scale,
                                           in1=tri384[:, :], op0=ALU.mult, op1=ALU.add).then_inc(sc_ev, 1)
                dve.wait_ge(sc_ev, 4 * n + 4)
                V.tensor_reduce(stat[:, 0:4], probs[:, :, 0:P], AX_X, ALU.max, negate=True)
                V.tensor_reduce(stat[:, 4:8], probs[:, :, P:384], AX_X, ALU.max, negate=True).then_inc(mx_ready, 1)

            def softmax_end(l, which):
                dve.wait_ge(ex_done, 2 * l + which + 1)
                link(V.reciprocal(stat[:, 8:16], stat[:, 8:16]))
                V.tensor_tensor(probs[:, :, 0:P], probs[:, :, 0:P],
                                stat[:, 8:12].unsqueeze(2).to_broadcast([P, HEADS, P]), ALU.mult)
                V.tensor_tensor(probs[:, :, P:384], probs[:, :, P:384],
                                stat[:, 12:16].unsqueeze(2).to_broadcast([P, HEADS, T]), ALU.mult).then_inc(pn_ready, 1)

            def probs_T_ev(l, which):
                n = 2 * l + which
                for hd in range(2, 4):
                    dve.wait_ge(pT_mm, 4 * n + hd + 1)
                    V.tensor_copy(pT[:, hd, :], bank[4 + hd][:, 0:384]).then_inc(pT_evV, 1)

            def o_lower(l, n, b):
                dve.wait_ge(o_hi[n], l + 1)
                V.tensor_tensor(oTl[:, n, :, :], bank[b][:, :].rearrange("p (c t) -> p c t", t=T),
                                oTh[:, n, :, :].bitcast(F32), ALU.subtract).then_inc(o_lo[n], 1)

            def a_norm(l):
                dve.wait_ge(prj_ev, n_chunk * l + 5)
                for m in range(MT):
                    V.bn_stats(stat[:, 46 + 6 * m:52 + 6 * m], prj[:, m, A_V:A_V + BW])
                link(V.engine_nop())
                for m in range(MT):
                    last = V.bn_aggr(stat[:, 40 + 2 * m:42 + 2 * m], stat[:, 46 + 6 * m:52 + 6 * m])
                link(last)
                V.tensor_copy(stat[:, 36:38], stat[:, 40:44:2]).then_inc(ams, 1)
                dve.wait_ge(ams_root, l + 1)
                link(V.reciprocal(stat[:, 38:40], stat[:, 40:44:2]))
                for m in range(MT):
                    v = prj[:, m, A_V:A_V + BW]
                    last = V.tensor_scalar(v, v, stat[:, 36 + m:37 + m], stat[:, 38 + m:39 + m], ALU.subtract, ALU.mult)
                link(last)
                v = prj[:, :, A_V:A_V + BW]
                link(V.tensor_tensor(v, v, again[:, 0, :].unsqueeze(1).to_broadcast([P, MT, BW]), ALU.mult))
                V.tensor_tensor(v, v, again[:, 1, :].unsqueeze(1).to_broadcast([P, MT, BW]),
                                ALU.add).then_inc(vln_ready, 1)

            def a_gate(l):
                dve.wait_ge(az_mm, l + 1)
                z = bank[4][:, :].rearrange("p (m c) -> p m c", m=MT)
                for g in range(4):
                    u = prj[:, :, A_U + HD * g:A_U + HD * (g + 1)]
                    last = V.scalar_tensor_tensor(out=u, in0=z[:, :, HD * g:HD * (g + 1)], scalar=abs_[:, g:g + 1],
                                                  in1=u, op0=ALU.add, op1=ALU.mult)
                last.then_inc(az_ev, 1)

            def glu(l):
                dve.wait_ge(glu_sig, l + 1)
                V.tensor_tensor(dxc[:, :, :], prj[:, :, D_A:D_A + BW], prj[:, :, D_G:D_G + BW],
                                ALU.mult).then_inc(glu_ready, 1)

            def conv_taps(l, first, n):
                if first == 0:
                    dve.wait_ge(zpad_ready, l + 1)
                for i in range(first, first + n):
                    j, c = i // 2, i % 2
                    if j:
                        dve.wait_ge(dve_seq, own[0] - 1)
                    z = zpad[:, c, j:j + T]
                    if j == 0:
                        ins = V.tensor_scalar(dacc[:, c, :], z, cw[:, c, 0:1], dcol[:, 0, c:c + 1], ALU.mult, ALU.add)
                    else:
                        ins = V.scalar_tensor_tensor(out=dacc[:, c, :], in0=z, scalar=cw[:, c, j:j + 1],
                                                     in1=dacc[:, c, :], op0=ALU.mult, op1=ALU.add)
                    own[0] += 1
                    ins.then_inc(dve_seq, 1)
                if first + n == 2 * D_CONV:
                    dve.wait_ge(dve_seq, own[0])
                    V.engine_nop().then_inc(conv_ready, 1)

            def d_center(l):
                dve.wait_ge(dmean_mm, l + 1)
                link(V.tensor_tensor(dxc[:, :, :], dacc[:, :, :],
                                     bank[7][:, 0:T].unsqueeze(1).to_broadcast([P, 2, T]), ALU.subtract))
                V.tensor_tensor(zpad[:, :, 0:T], dxc[:, :, :], dxc[:, :, :], ALU.mult).then_inc(dsq_ready, 1)

            def d_finish(l):
                dve.wait_ge(dms_root, l + 1)
                link(V.reciprocal(dsd, dsd))
                link(V.tensor_tensor(dxc[:, :, :], dxc[:, :, :], dsd.unsqueeze(1).to_broadcast([P, 2, T]), ALU.mult))
                for c in range(2):
                    last = V.tensor_scalar(dxc[:, c, :], dxc[:, c, :], dcol[:, 1, c:c + 1], dcol[:, 2, c:c + 1],
                                           ALU.mult, ALU.add)
                last.then_inc(dlin_ready, 1)
                dve.wait_ge(dsig_ready, l + 1)
                V.tensor_tensor(dacc[:, :, :], dxc[:, :, :], zpad[:, :, 0:T], ALU.mult).then_inc(do_ready, 1)

            def merge(l, n, pc):
                dve.wait_ge(gate_sig, 2 * (NB * l + n + 1))
                for c in range(2):
                    dve.wait_ge(w_used, 2 * pc.number + c + 1)
                    for m in range(MT):
                        g = gates[:, m, D * n + 512 * c:D * n + 512 * (c + 1)]
                        y = hm[:, m, 512 * c:512 * (c + 1)]
                        b = bank[4 * (n % 2) + 2 * c + m][:, :]
                        if n == 0:
                            V.tensor_tensor(y, g, b, ALU.mult).then_inc(br_ev, 1)
                        else:
                            link(V.tensor_tensor(g, g, b, ALU.mult))
                            V.tensor_tensor(y, y, g, ALU.add).then_inc(br_ev, 1)

            def mixer(l):
                pcs = mixer_pieces(l)
                taps = {13: (0, 6), 14: (6, 4), 15: (10, 4), 16: (14, 6), 17: (20, 6), 18: (26, 8), 19: (34, 8),
                        20: (42, 8), 21: (50, 8), 22: (58, 4)}
                for s in range(MIX_PIECES):
                    if s == 28:
                        merge(l, 3, pcs[s])
                        lower_hT(yT_lo, yT_hi, lambda m, g: 4 * l + 2 * g + m + 1, (0,))
                    if s + 2 < MIX_PIECES:
                        split_lo(dve, pcs[s + 2], piece_half(s + 2))
                    elif s + 2 == MIX_PIECES:
                        split_lo(dve, after_mixer(l, 0))
                    if s == 2:
                        prep(l)
                    if s == 3:
                        c_norm_latents(l)
                    if s == 6:
                        c_sum_qk(l)
                    if s == 7:
                        c_rotate_qk(l)
                    if s == 8:
                        a_norm(l)
                        dve.wait_ge(qT_mm, 4 * l + 2)
                        for c in range(2):
                            last = V.tensor_copy(qkT[0:C_QK, 1, 2 * c:2 * c + 2, :],
                                                 bank[6 + c][0:C_QK, :].rearrange("p (h t) -> p h t", t=T))
                        last.then_inc(qT_evV, 1)
                    if s == 9:
                        softmax_start(l, 0)
                    if s == 10:
                        softmax_end(l, 0)
                    if s == 11:
                        probs_T_ev(l, 0)
                        glu(l)
                        b_sum_qk(l)
                    if s == 12:
                        o_lower(l, 2, 4)
                        b_rotate_qk(l)
                    if s == 13:
                        dve.wait_ge(qT_mm, 4 * l + 4)
                        V.tensor_copy(qkT[:, 0, 2:4, :],
                                      bank[5][:, :].rearrange("p (h t) -> p h t", t=T)).then_inc(qT_evV, 1)
                    if s == 14:
                        softmax_start(l, 1)
                    if s == 15:
                        softmax_end(l, 1)
                        a_gate(l)
                    if s == 16:
                        probs_T_ev(l, 1)
                    if s == 17:
                        o_lower(l, 1, 4)
                        o_lower(l, 0, 6)
                    if s in taps:
                        conv_taps(l, *taps[s])
                    if s == 23:
                        d_center(l)
                    if s == 24:
                        d_finish(l)
                    if s == 26:
                        dve.wait_ge(o_hi[3], l + 1)
                        V.tensor_tensor(oTl[:, 3, :, :], dacc[:, :, :], oTh[:, 3, :, :].bitcast(F32),
                                        ALU.subtract).then_inc(o_lo[3], 1)
                    if 25 <= s < 28:
                        merge(l, s - 25, pcs[s])
                    if s == 29:
                        lower_hT(yT_lo, yT_hi, lambda m, g: 4 * l + 2 * g + m + 1, (1,))
                V.engine_nop().then_inc(layer_done, 1)

            def swiglu(m, b, n, e_done, e_count, out_sem, scaled=False):
                s = sig[:, m, 0:n]
                r = rstd[:, 1, m:m + 1]
                if scaled:
                    V.scalar_tensor_tensor(out=s, in0=b[:, 0:n], scalar=r, in1=s, op0=ALU.mult,
                                           op1=ALU.mult).then_inc(e_done, 1)
                else:
                    V.tensor_tensor(s, s, b[:, 0:n], ALU.mult).then_inc(e_done, 1)
                dve.wait_ge(e_done, e_count)
                if scaled:
                    ins = V.scalar_tensor_tensor(out=act[:, m, 0:n], in0=b[:, n:2 * n], scalar=r, in1=s, op0=ALU.mult,
                                                 op1=ALU.mult)
                else:
                    ins = V.tensor_tensor(act[:, m, 0:n], s, b[:, n:2 * n], ALU.mult)
                if out_sem is not None:
                    ins.then_inc(out_sem, 1)

            def ffn():
                def gated(i):
                    for m in range(MT):
                        dve.wait_ge(sig_ready, 2 * i + m + 1)
                        swiglu(m, bank[4 + m], FSTEP, silu_ready, 2 * i + m + 1,
                               act_ready if m else None, scaled=True)

                def turned(i, par):
                    dve.wait_ge(aT_hi, i + 1)
                    V.tensor_tensor(aTl[par][:, :, :], bank[6 + par][:, :].rearrange("p (k t) -> p k t", t=T),
                                    aTh[par][:, :, :].bitcast(F32), ALU.subtract).then_inc(aT_lo, 1)

                def body(i, par, first, it, per, ahead=True):
                    split_lo(dve, Piece(first + 1, it, per))
                    split_lo(dve, Piece(first + 2, it, per))
                    gated(i)
                    if ahead:
                        split_lo(dve, Piece(first + 3, it, per))
                    turned(i, par)

                dve.wait_ge(rstd_ready, 2)
                gated(0)
                split_lo(dve, Piece(FFN_BASE + 2))
                turned(0, 0)
                with dve.Fori(0, 4) as it:
                    for r in range(2):
                        body(2 * it + 1 + r, (1 + r) % 2, FFN_BASE + 2 + 3 * r, it, 6)
                body(9, 1, FFN_BASE + 26, 0, 0)
                body(10, 0, FFN_BASE + 29, 0, 0, ahead=False)
                split_lo(dve, Piece(FFN_BASE + 32))
                split_lo(dve, Piece(FFN_BASE + 33))

            def router_prep():
                dve.wait_ge(iota_ready, 1)
                V.tensor_copy(iotaf[:, :], iotai[:, :])
                V.memset(tab[:, :, :], 0.0)
                dve.wait_ge(wr_hi, 1)
                V.tensor_tensor(wrl[:, :, :], wr[:, :, :], wrh[:, :, :].bitcast(F32), ALU.subtract).then_inc(wr_lo, 1)

            def router():
                dve.wait_ge(lgT_mm, 1)
                dve.wait_ge(rstd_ready, 4)
                for m in range(MT):
                    last = V.scalar_tensor_tensor(out=lg[:, m, :], in0=bank[6][:, 32 + 8 * m:40 + 8 * m],
                                                  scalar=rstd[:, 1, m:m + 1], in1=rbias[:, :], op0=ALU.mult, op1=ALU.add)
                link(last)
                for m in range(MT):
                    last = V.max(top8[:, m, :], lg[:, m, :])
                link(last)
                for s in range(2):
                    last = V.tensor_tensor(diff[:, :, s:s + 1], top8[:, :, s:s + 1], top8[:, :, 1 - s:2 - s],
                                           ALU.subtract)
                last.then_inc(diff_ready, 1)
                for m in range(MT):
                    last = V.max_index(idx8[:, m, :], top8[:, m, :], lg[:, m, :])
                link(last)
                link(V.tensor_copy(idxf[:, :, :], idx8[:, :, 0:2]))
                for s in range(2):
                    for m in range(MT):
                        last = V.tensor_scalar(hot[:, s, m, :], iotaf[:, 0:NE], idxf[:, m, s:s + 1], None, ALU.is_equal)
                link(last)
                V.tensor_tensor(tab[:, 2:4, 0:NE], hot[:, 0, :, :], hot[:, 1, :, :], ALU.add).then_inc(member_ready, 1)
                for m in range(MT):
                    dve.wait_ge(tok_hi, m + 1)
                    V.scalar_tensor_tensor(out=htokl[:, m, :], in0=hm[:, m, :], scalar=rstd[:, 1, m:m + 1],
                                           in1=htokh[:, m, :].bitcast(F32), op0=ALU.mult,
                                           op1=ALU.subtract).then_inc(tok_lo, 1)
                dve.wait_ge(member_ready, 1)
                dve.wait_ge(wtop_ready, 1)
                for m in range(MT):
                    last = V.tensor_scalar(hot[:, 0, m, :], hot[:, 0, m, :], wtop[:, m, 0:1], None, ALU.mult)
                link(last)
                for m in range(MT):
                    V.scalar_tensor_tensor(out=tab[:, 4 + m, 0:NE], in0=hot[:, 1, m, :], scalar=wtop[:, m, 1:2],
                                           in1=hot[:, 0, m, :], op0=ALU.mult, op1=ALU.add)
                dve.wait_ge(rank_mm, 1)
                V.tensor_copy(tab[:, 0:2, 0:NE], bank[6][:, 0:16].rearrange("p (m e) -> p m e", m=MT))
                V.tensor_copy(cnt[:, :], bank[6][:, 16:24])
                link(V.engine_nop())

            def second_passes():
                link(V.tensor_scalar(over[:, :], cnt[:, :], float(SLOTS), None, ALU.is_gt))
                link(V.tensor_tensor(prefix[:, :, :], before_e[:, :, :],
                                     over[:, :].unsqueeze(1).to_broadcast([P, NE, NE]), ALU.mult))
                V.tensor_copy(eidf[:, :], iotaf[:, 0:PASSES])
                link(V.tensor_reduce(oidx[:, :], prefix[:, :, :], AX_X, ALU.add))
                V.tensor_scalar(lastf[:, :], oidx[:, NE - 1:NE], over[:, NE - 1:NE], float(NE - 1), ALU.add, ALU.add)
                for o in range(3):
                    last = V.scalar_tensor_tensor(out=sel[:, o, :], in0=oidx[:, :], scalar=float(o), in1=over[:, :],
                                                  op0=ALU.is_equal, op1=ALU.mult)
                link(last)
                V.tensor_copy(lasti[:, :], lastf[:, :])
                V.tensor_tensor(eprod[:, :, :], sel[:, :, :], iotaf[:, 0:NE].unsqueeze(1).to_broadcast([P, 3, NE]),
                                ALU.mult)
                for o in range(3):
                    last = V.tensor_tensor(prod[:, o, :, :], tab[:, :, 0:NE],
                                           sel[:, o, :].unsqueeze(1).to_broadcast([P, 6, NE]), ALU.mult)
                link(last)
                V.tensor_reduce(eidf[:, NE:NE + 3], eprod[:, :, :], AX_X, ALU.add)
                link(V.tensor_reduce(tab[:, :, NE:NE + 3].rearrange("p r o -> p o r"), prod[:, :, :, :], AX_X, ALU.add))
                V.tensor_scalar(tab[:, 0:2, NE:NE + 3], tab[:, 0:2, NE:NE + 3], float(SLOTS), None, ALU.subtract)
                link(V.tensor_copy(eidi[:, :], eidf[:, :]))
                V.engine_nop().then_inc(tab_ready, 1)

            def expert_pass(p, before=None):
                first = before is None
                def pc(j):
                    return Piece(MOE_BASE + j, p, PASS_PIECES, experts=True)

                def half(j):
                    return ESTEPS[ORDER[j][1]] * 4

                def turned(s):
                    dve.wait_ge(e_aT_hi, 6 * p + s + 1)
                    nk = ESTEPS[s] // P
                    V.tensor_tensor(aTl[s % 2][:, 0:nk, 0:P], bank[4][:, 0:ESTEPS[s]].rearrange("p (k t) -> p k t", t=P),
                                    aTh[s % 2][:, 0:nk, 0:P].bitcast(F32), ALU.subtract).then_inc(e_aT_lo, 1)

                if not first:
                    split_lo(dve, pc(0))
                    split_lo(dve, pc(1))
                    rows_lower(before)
                for j, (kind, s) in enumerate(ORDER):
                    if kind == "u":
                        dve.wait_ge(e_sig, 6 * p + s + 1)
                        swiglu(0, bank[2 + s % 2], ESTEPS[s], e_silu, 6 * p + s + 1, e_act)
                    if j + 2 < PASS_PIECES:
                        split_lo(dve, pc(j + 2), half(j + 2))
                    if kind == "u" and s == 0:
                        turned(0)
                    if j == 2:
                        if not first:
                            scattered(before, 0)
                        dve.wait_ge(pickT_ev, p + 1)
                        V.tensor_copy(wslot[:, :], bank[7][:, T:T + 1]).then_inc(wslot_ready, 1)
                    if j == 7 and not first:
                        scattered(before, 1)
                    if j == 9:
                        pick_slots(p + 1)
                    if j == 10 and first:
                        second_passes()
                    if kind == "u" and s == 5:
                        gathered_lower(p + 1, (0,))
                    if kind == "d" and s < 5:
                        turned(s + 1)
                    if j == PASS_PIECES - 2:
                        gathered_lower(p + 1, (1,))

            def pick_slots(q):
                for m in range(MT):
                    rank = tab[:, m, bass.ds(q, 1)]
                    member = tab[:, 2 + m, bass.ds(q, 1)]
                    V.tensor_scalar(pick[:, m, :], iotaf[:, :], rank, member, ALU.is_equal, ALU.mult)
                    V.tensor_scalar(pickf[:, m, :], iotaf[:, :], rank, member, ALU.is_equal, ALU.mult)
                    last = V.tensor_copy(wcol[:, m:m + 1], tab[:, 4 + m, bass.ds(q, 1)])
                last.then_inc(pick_ready, 1)

            def gathered_lower(q, halves=(0, 1)):
                for g in halves:
                    dve.wait_ge(gat_hi, 2 * q + g + 1)
                    V.tensor_tensor(xgl[:, 4 * g:4 * g + 4, :], bank[5 + g][:, :].rearrange("p (k t) -> p k t", t=P),
                                    xgh[:, 4 * g:4 * g + 4, :].bitcast(F32), ALU.subtract).then_inc(gat_lo, 1)

            def rows_lower(q):
                for c in range(2):
                    dve.wait_ge(y_hi, 2 * q + c + 1)
                    o = slice(512 * c, 512 * (c + 1))
                    V.scalar_tensor_tensor(out=yl[:, o], in0=bank[c][:, :], scalar=wslot[:, 0:1],
                                           in1=yh[:, o].bitcast(F32), op0=ALU.mult, op1=ALU.subtract).then_inc(y_lo, 1)

            def scattered(q, m):
                for c in range(2):
                    dve.wait_ge(sca_mm, 4 * q + 2 * m + c + 1)
                    o = x[:, m, 512 * c:512 * (c + 1)]
                    V.tensor_tensor(o, o, bank[(0, 5)[m] + c][:, :], ALU.add).then_inc(sca_add, 1)

            token_norm(0)
            dve.wait_ge(const_ready, 1)
            dve.wait_ge(pos_in, 16)
            angles()
            mixer(0)
            token_norm(1, Piece(MIX_PIECES - 1), 1, after_mixer(0, 1))
            router_prep()
            ffn()
            token_norm(2, Piece(FFN_BASE + 32), 2, Piece(FFN_BASE + 34))
            mixer(1)
            token_norm(3, mixer_pieces(1)[-1], 3, after_mixer(1, 1))
            router()
            pick_slots(0)
            gathered_lower(0)
            expert_pass(0)
            dve.wait_ge(tab_ready, 1)
            last_pass = dve.value_load(lasti[0:1, 0:1], min_val=NE - 1, max_val=PASSES - 2)
            with dve.Fori(0, last_pass) as r:
                expert_pass(r + 1, before=r)
            rows_lower(last_pass)
            for m in range(MT):
                scattered(last_pass, m)


def kernel(**inputs):
    import concourse.bacc as bacc
    from concourse.bass_utils import run_bass_kernel_spmd

    nc = bacc.Bacc("TRN2", target_bir_lowering=False, num_devices=1)
    arrays, aps = {}, {}
    for name in INPUTS:
        v = np.ascontiguousarray(inputs[name])
        arrays[f"in_{name}"] = v
        aps[name] = nc.dram_tensor(f"in_{name}", v.shape, mybir.dt.from_np(v.dtype), kind="ExternalInput").ap()
    out = nc.dram_tensor("out_x", (1, T, D), F32, kind="ExternalOutput").ap()
    build_trunk(nc, aps, out)
    r = run_bass_kernel_spmd(nc, [arrays], core_ids=[0])
    return r.results[0]["out_x"]
```
